# Optimizing a Trainium2 kernel written in Bass

```python
import jax
import jax.numpy as jnp
from jax import lax
import numpy as np
import math
import jax, jax.numpy as jnp

D_MODEL = 2048
BATCH = 1
SEQ = 256
DEPTH = 2

GRID_W = 64
CTX_LEN = 256
EPS = 1e-6

NA_HEADS = 16
NA_HEAD_DIM = 128
NA_WIDTH = NA_HEADS * NA_HEAD_DIM
NA_KH = 8
NA_KW = 16

SSD_HEAD_DIM = 64
SSD_WIDTH = D_MODEL
SSD_HEADS = SSD_WIDTH // SSD_HEAD_DIM
SSD_GROUPS = 8
SSD_HPG = SSD_HEADS // SSD_GROUPS
SSD_STATE = 128
SSD_CONV = 5
SSD_CHUNK = 128
SSD_XBC = SSD_WIDTH + 2 * SSD_GROUPS * SSD_STATE

SC_WIDTH = D_MODEL
SC_CONV = 3

MIX_WIDTH = NA_WIDTH + SSD_WIDTH
COL_Q = 0
COL_GATE_A = COL_Q + NA_WIDTH
COL_Z = COL_GATE_A + NA_WIDTH
COL_K = COL_Z + SSD_WIDTH
COL_V = COL_K + NA_WIDTH
COL_XBC = COL_V + NA_WIDTH
COL_DT = COL_XBC + SSD_XBC
EVEN_IN = COL_DT + 2 * SSD_HEADS
ODD_IN = 4 * SC_WIDTH
N_EVEN = (DEPTH + 1) // 2
N_ODD = DEPTH // 2


def rms_norm(x, g):
    xf = x.astype(jnp.float32)
    y = xf * lax.rsqrt(jnp.mean(xf * xf, axis=-1, keepdims=True) + EPS)
    return (y * g.astype(jnp.float32)).astype(x.dtype)

def adaln(cond, w, b):
    m = jax.nn.silu(cond) @ w + b
    return jnp.split(m, 3, axis=-1)

def modulate(h, shift, scale):
    return h * (1 + scale) + shift

def cols(p, start, width, base):
    return p[..., start - base:start - base + width]

def heads(t, n, d):
    return t.reshape(*t.shape[:2], n, d)

def dw_conv(x, w, b=None):
    k = w.shape[0]
    y = lax.conv_general_dilated(x, w[:, None, :], window_strides=(1,), padding=[(k // 2, k // 2)],
                                 dimension_numbers=('NWC', 'WIO', 'NWC'), feature_group_count=x.shape[-1])
    return y if b is None else y + b

def neighbourhood_attention(q, k, v, k_ctx, v_ctx, rpb):
    b, seq, nh, dh = q.shape
    rows = seq // GRID_W
    kh = min(NA_KH, rows)
    scale = dh ** -0.5
    qg = q.reshape(b, rows, GRID_W, nh, dh)
    kg = k.reshape(b, rows, GRID_W, nh, dh)
    vg = v.reshape(b, rows, GRID_W, nh, dh)
    col = jnp.arange(GRID_W)
    col_start = jnp.clip(col - NA_KW // 2, 0, GRID_W - NA_KW)
    in_win = (col[None, :] >= col_start[:, None]) & (col[None, :] < col_start[:, None] + NA_KW)
    mask = jnp.broadcast_to(in_win[:, None, :], (GRID_W, kh, GRID_W)).reshape(GRID_W, kh * GRID_W)
    dc_idx = jnp.clip(col[None, :] - col[:, None], -(NA_KW - 1), NA_KW - 1) + NA_KW - 1

    def row_block(r):
        rs = jnp.clip(r - kh // 2, 0, rows - kh)
        qr = lax.dynamic_index_in_dim(qg, r, axis=1, keepdims=False)
        kb = lax.dynamic_slice_in_dim(kg, rs, kh, axis=1).reshape(b, kh * GRID_W, nh, dh)
        vb = lax.dynamic_slice_in_dim(vg, rs, kh, axis=1).reshape(b, kh * GRID_W, nh, dh)
        dr_idx = rs + jnp.arange(kh) - r + NA_KH - 1
        bias = rpb[:, dr_idx[None, :, None], dc_idx[:, None, :]].reshape(nh, GRID_W, kh * GRID_W)
        s_lat = jnp.einsum('bqhd,bkhd->bhqk', qr, kb).astype(jnp.float32) * scale + bias.astype(jnp.float32)
        s_lat = jnp.where(mask, s_lat, -jnp.inf)
        s_ctx = jnp.einsum('bqhd,bkhd->bhqk', qr, k_ctx).astype(jnp.float32) * scale
        pr = jax.nn.softmax(jnp.concatenate([s_lat, s_ctx], axis=-1), axis=-1).astype(v.dtype)
        return (jnp.einsum('bhqk,bkhd->bqhd', pr[..., :kh * GRID_W], vb)
                + jnp.einsum('bhqk,bkhd->bqhd', pr[..., kh * GRID_W:], v_ctx))

    out = lax.map(row_block, jnp.arange(rows))
    return jnp.moveaxis(out, 0, 1).reshape(b, seq, nh, dh)

def context_attention(q, k, v):
    s = jnp.einsum('bqhd,bkhd->bhqk', q, k).astype(jnp.float32) * q.shape[-1] ** -0.5
    pr = jax.nn.softmax(s, axis=-1).astype(v.dtype)
    return jnp.einsum('bhqk,bkhd->bqhd', pr, v)

def ssd_scan(x, dt, a, bm, cm, h0):
    b, seq = x.shape[:2]
    nc = seq // SSD_CHUNK

    def chunks(t):
        return jnp.moveaxis(t.reshape(b, nc, SSD_CHUNK, *t.shape[2:]), 1, 0)

    tri = jnp.tril(jnp.ones((SSD_CHUNK, SSD_CHUNK), bool))[None, :, :, None, None]

    def step(h, inp):
        xc, dtc, bc, cc = inp
        cs = jnp.cumsum(dtc * a, axis=1)
        seg = cs[:, :, None] - cs[:, None, :]
        decay = jnp.exp(jnp.where(tri, seg, -jnp.inf))
        cb = jnp.einsum('bign,bjgn->bijg', cc, bc)
        w = cb[..., None] * decay * dtc[:, None]
        y = jnp.einsum('bijgr,bjgrp->bigrp', w, xc)
        y = y + jnp.einsum('bign,bgrpn->bigrp', cc, h) * jnp.exp(cs)[..., None]
        to_end = jnp.exp(cs[:, -1:] - cs) * dtc
        h = h * jnp.exp(cs[:, -1])[..., None, None] + jnp.einsum('bjgn,bjgr,bjgrp->bgrpn', bc, to_end, xc)
        return h, y

    h, ys = lax.scan(step, h0, (chunks(x), chunks(dt), chunks(bm), chunks(cm)))
    return jnp.moveaxis(ys, 0, 1).reshape(x.shape), h

def ssd_final_state(x, dt, a, bm):
    cs = jnp.cumsum(dt * a, axis=1)
    to_end = jnp.exp(cs[:, -1:] - cs) * dt
    return jnp.einsum('bjgn,bjgr,bjgrp->bgrpn', bm, to_end, x)

def _flip(t, rev):
    return jnp.flip(t, axis=1) if rev else t

def bidirectional_ssd(lat, con, a, want_ctx):
    xs, dt, bm, cm = lat
    xs_c, dt_c, bm_c, cm_c = con
    b = xs.shape[0]
    y = jnp.zeros_like(xs)
    yc = jnp.zeros_like(xs_c) if want_ctx else None
    for d in range(2):
        rev = d == 1
        if want_ctx:
            h0 = jnp.zeros((b, SSD_GROUPS, SSD_HPG, SSD_HEAD_DIM, SSD_STATE), jnp.float32)
            yc_d, hc = ssd_scan(_flip(xs_c, rev), _flip(dt_c[:, :, d], rev), a[d], _flip(bm_c, rev), _flip(cm_c, rev), h0)
            yc = yc + _flip(yc_d, rev)
        else:
            hc = ssd_final_state(_flip(xs_c, rev), _flip(dt_c[:, :, d], rev), a[d], _flip(bm_c, rev))
        y_d, _ = ssd_scan(_flip(xs, rev), _flip(dt[:, :, d], rev), a[d], _flip(bm, rev), _flip(cm, rev), hc)
        y = y + _flip(y_d, rev)
    return y, yc

def ssd_inputs(p, base, conv_w, conv_b, dt_bias):
    b, seq = p.shape[:2]
    gn = SSD_GROUPS * SSD_STATE
    xbc = jax.nn.silu(dw_conv(cols(p, COL_XBC, SSD_XBC, base), conv_w, conv_b)).astype(jnp.float32)
    xs = xbc[..., :SSD_WIDTH].reshape(b, seq, SSD_GROUPS, SSD_HPG, SSD_HEAD_DIM)
    bm = xbc[..., SSD_WIDTH:SSD_WIDTH + gn].reshape(b, seq, SSD_GROUPS, SSD_STATE)
    cm = xbc[..., SSD_WIDTH + gn:].reshape(b, seq, SSD_GROUPS, SSD_STATE)
    dt_raw = cols(p, COL_DT, 2 * SSD_HEADS, base).astype(jnp.float32).reshape(b, seq, 2, SSD_GROUPS, SSD_HPG)
    dt = jax.nn.softplus(dt_raw + dt_bias.astype(jnp.float32).reshape(2, SSD_GROUPS, SSD_HPG))
    return xs, dt, bm, cm

def gated_group_rmsnorm(y, z, g):
    b, seq = y.shape[:2]
    yz = (y.reshape(b, seq, SSD_WIDTH) * jax.nn.silu(z.astype(jnp.float32))).reshape(b, seq, SSD_GROUPS, -1)
    yz = yz * lax.rsqrt(jnp.mean(yz * yz, axis=-1, keepdims=True) + EPS)
    return (yz.reshape(b, seq, SSD_WIDTH) * g.astype(jnp.float32)).astype(z.dtype)

def na_ssd_mixer(h, hc, w_in, conv_w, conv_b, a_log, dt_bias, d_skip, ssm_norm_g,
                 q_norm_g, k_norm_g, rpb, w_out, update_ctx):
    b, seq, _ = h.shape
    p = h @ w_in
    base = 0 if update_ctx else COL_K
    pc = hc @ w_in[:, base:]
    q = rms_norm(heads(cols(p, COL_Q, NA_WIDTH, 0), NA_HEADS, NA_HEAD_DIM), q_norm_g)
    k = rms_norm(heads(cols(p, COL_K, NA_WIDTH, 0), NA_HEADS, NA_HEAD_DIM), k_norm_g)
    v = heads(cols(p, COL_V, NA_WIDTH, 0), NA_HEADS, NA_HEAD_DIM)
    kc = rms_norm(heads(cols(pc, COL_K, NA_WIDTH, base), NA_HEADS, NA_HEAD_DIM), k_norm_g)
    vc = heads(cols(pc, COL_V, NA_WIDTH, base), NA_HEADS, NA_HEAD_DIM)
    ya = neighbourhood_attention(q, k, v, kc, vc, rpb).reshape(b, seq, NA_WIDTH)
    ya = ya * jax.nn.silu(cols(p, COL_GATE_A, NA_WIDTH, 0))
    a = -jnp.exp(a_log.astype(jnp.float32)).reshape(2, SSD_GROUPS, SSD_HPG)
    d = d_skip.astype(jnp.float32).reshape(SSD_GROUPS, SSD_HPG)[..., None]
    lat = ssd_inputs(p, 0, conv_w, conv_b, dt_bias)
    con = ssd_inputs(pc, base, conv_w, conv_b, dt_bias)
    y_ssd, yc_ssd = bidirectional_ssd(lat, con, a, update_ctx)
    yb = gated_group_rmsnorm(y_ssd + d * lat[0], cols(p, COL_Z, SSD_WIDTH, 0), ssm_norm_g)
    out = jnp.concatenate([ya, yb], axis=-1) @ w_out
    out_c = None
    if update_ctx:
        n_ctx = hc.shape[1]
        qc = rms_norm(heads(cols(pc, COL_Q, NA_WIDTH, 0), NA_HEADS, NA_HEAD_DIM), q_norm_g)
        yac = context_attention(qc, kc, vc).reshape(b, n_ctx, NA_WIDTH) * jax.nn.silu(cols(pc, COL_GATE_A, NA_WIDTH, 0))
        ybc = gated_group_rmsnorm(yc_ssd + d * con[0], cols(pc, COL_Z, SSD_WIDTH, 0), ssm_norm_g)
        out_c = jnp.concatenate([yac, ybc], axis=-1) @ w_out
    return out, out_c

def short_conv_mixer(h, w_in, conv_w, w_out):
    p = h @ w_in
    bg, cg, hv, g = jnp.split(p, 4, axis=-1)
    y = bg * dw_conv(cg * hv, conv_w)
    return (jax.nn.silu(g) * y) @ w_out

def first_inputs(seed: int = 0) -> dict:
    key = jax.random.key(seed)
    ks = jax.random.split(key, 21)
    nrm = jax.random.normal
    dt0 = jnp.exp(jax.random.uniform(ks[11], (N_EVEN, 2, SSD_HEADS), minval=float(np.log(1e-3)), maxval=float(np.log(1e-1))))
    return {
        'x': nrm(ks[0], (BATCH, SEQ, D_MODEL), jnp.float32),
        'c': nrm(ks[1], (BATCH, D_MODEL), jnp.float32),
        'ctx': nrm(ks[2], (BATCH, CTX_LEN, D_MODEL), jnp.float32),
        'c_ctx': nrm(ks[3], (D_MODEL,), jnp.float32),
        'ada_w': nrm(ks[4], (DEPTH, D_MODEL, 3 * D_MODEL), jnp.float32) * (0.5 * D_MODEL ** -0.5),
        'ada_b': nrm(ks[5], (DEPTH, 3 * D_MODEL), jnp.float32) * 0.02,
        'norm_g': 1.0 + 0.05 * nrm(ks[6], (DEPTH, D_MODEL), jnp.float32),
        'na_ssd_w_in': nrm(ks[7], (N_EVEN, D_MODEL, EVEN_IN), jnp.float32) * D_MODEL ** -0.5,
        'ssd_conv_w': nrm(ks[8], (N_EVEN, SSD_CONV, SSD_XBC), jnp.float32) * SSD_CONV ** -0.5,
        'ssd_conv_b': nrm(ks[9], (N_EVEN, SSD_XBC), jnp.float32) * 0.02,
        'ssd_a_log': jnp.log(jax.random.uniform(ks[10], (N_EVEN, 2, SSD_HEADS), minval=1.0, maxval=16.0)),
        'ssd_dt_bias': dt0 + jnp.log(-jnp.expm1(-dt0)),
        'ssd_d': 1.0 + 0.1 * nrm(ks[12], (N_EVEN, SSD_HEADS), jnp.float32),
        'ssd_norm_g': 1.0 + 0.05 * nrm(ks[13], (N_EVEN, SSD_WIDTH), jnp.float32),
        'q_norm_g': 1.0 + 0.05 * nrm(ks[14], (N_EVEN, NA_HEAD_DIM), jnp.float32),
        'k_norm_g': 1.0 + 0.05 * nrm(ks[15], (N_EVEN, NA_HEAD_DIM), jnp.float32),
        'na_rpb': nrm(ks[16], (N_EVEN, NA_HEADS, 2 * NA_KH - 1, 2 * NA_KW - 1), jnp.float32) * 0.1,
        'na_ssd_w_out': nrm(ks[17], (N_EVEN, MIX_WIDTH, D_MODEL), jnp.float32) * MIX_WIDTH ** -0.5,
        'sc_w_in': nrm(ks[18], (N_ODD, D_MODEL, ODD_IN), jnp.float32) * D_MODEL ** -0.5,
        'sc_conv_w': nrm(ks[19], (N_ODD, SC_CONV, SC_WIDTH), jnp.float32) * SC_CONV ** -0.5,
        'sc_w_out': nrm(ks[20], (N_ODD, SC_WIDTH, D_MODEL), jnp.float32) * SC_WIDTH ** -0.5,
    }

def first_block(x, c, ctx, c_ctx, ada_w, ada_b, norm_g, na_ssd_w_in, ssd_conv_w, ssd_conv_b,
              ssd_a_log, ssd_dt_bias, ssd_d, ssd_norm_g, q_norm_g, k_norm_g, na_rpb,
              na_ssd_w_out, sc_w_in, sc_conv_w, sc_w_out):
    for i in range(DEPTH):
        update_ctx = any(j % 2 == 0 for j in range(i + 1, DEPTH))
        needs_ctx = (i % 2 == 0) or update_ctx
        shift, scale, gate = adaln(c, ada_w[i], ada_b[i])
        h = modulate(rms_norm(x, norm_g[i]), shift[:, None], scale[:, None])
        if needs_ctx:
            shift_c, scale_c, gate_c = adaln(c_ctx, ada_w[i], ada_b[i])
            hc = modulate(rms_norm(ctx, norm_g[i]), shift_c, scale_c)
        if i % 2 == 0:
            e = i // 2
            y, yc = na_ssd_mixer(h, hc, na_ssd_w_in[e], ssd_conv_w[e], ssd_conv_b[e], ssd_a_log[e],
                                 ssd_dt_bias[e], ssd_d[e], ssd_norm_g[e], q_norm_g[e], k_norm_g[e],
                                 na_rpb[e], na_ssd_w_out[e], update_ctx)
        else:
            o = i // 2
            y = short_conv_mixer(h, sc_w_in[o], sc_conv_w[o], sc_w_out[o])
            yc = short_conv_mixer(hc, sc_w_in[o], sc_conv_w[o], sc_w_out[o]) if update_ctx else None
        x = x + gate[:, None] * y
        if update_ctx:
            ctx = ctx + gate_c * yc
    return x


DEPTH_2 = 1

CHUNK = 64
Q_BLOCK = 128
HEAD_DIM = 128
D_MIX = D_MODEL
D_SB = D_MIX // 2
D_CH = D_MIX - D_SB
N_HEADS_SB = D_SB // HEAD_DIM
N_HEADS_CH = D_CH // HEAD_DIM
LEFT_CHUNKS = 8
BAND = LEFT_CHUNKS + 1
REL_CLIP = 256
N_REL = REL_CLIP + CHUNK
D_IN = 4 * D_SB + 4 * D_CH
NORM_EPS = 1e-6
NEG_BIG = -1e30


def rms_norm_2(x, g):
    xf = x.astype(jnp.float32)
    y = xf * lax.rsqrt(jnp.mean(xf * xf, axis=-1, keepdims=True) + NORM_EPS)
    return (y * g.astype(jnp.float32)).astype(x.dtype)

def split_heads(t, n_heads):
    b, s, _ = t.shape
    return t.reshape(b, s, n_heads, HEAD_DIM).transpose(0, 2, 1, 3)

def merge_heads(t):
    b, h, s, d = t.shape
    return t.transpose(0, 2, 1, 3).reshape(b, s, h * d)

def stick_breaking_attention(q, k, v):
    seq = q.shape[2]
    scale = q.shape[-1] ** -0.5
    outs = []
    for blk in range(seq // Q_BLOCK):
        t0 = blk * Q_BLOCK
        t1 = t0 + Q_BLOCK
        qb = q[:, :, t0:t1]
        kb = k[:, :, :t1]
        vb = v[:, :, :t1]
        z = jnp.einsum('bhtd,bhsd->bhts', qb, kb).astype(jnp.float32) * scale
        t_idx = jnp.arange(t0, t1)[:, None]
        s_idx = jnp.arange(t1)[None, :]
        causal = s_idx < t_idx
        log_stay = jnp.where(causal, jax.nn.log_sigmoid(-z), 0.0)
        after = lax.cumsum(log_stay, axis=3, reverse=True) - log_stay
        w = jnp.where(causal, jnp.exp(jax.nn.log_sigmoid(z) + after), 0.0)
        outs.append(jnp.einsum('bhts,bhsd->bhtd', w.astype(v.dtype), vb))
    return jnp.concatenate(outs, axis=2)

def chunk_band_attention(q, k, v, q_gain, k_gain, rel_table):
    b, h, seq, d = q.shape
    nc = seq // CHUNK
    q = rms_norm_2(q, q_gain)
    k = rms_norm_2(k, k_gain)
    qc = q.reshape(b, h, nc, CHUNK, d)
    pad = ((0, 0), (0, 0), (LEFT_CHUNKS * CHUNK, 0), (0, 0))
    kc = jnp.pad(k, pad).reshape(b, h, nc + LEFT_CHUNKS, CHUNK, d)
    vc = jnp.pad(v, pad).reshape(b, h, nc + LEFT_CHUNKS, CHUNK, d)
    band_idx = jnp.arange(nc)[:, None] + jnp.arange(BAND)[None, :]
    kband = kc[:, :, band_idx].reshape(b, h, nc, BAND * CHUNK, d)
    vband = vc[:, :, band_idx].reshape(b, h, nc, BAND * CHUNK, d)
    scores = jnp.einsum('bhcid,bhcpd->bhcip', qc, kband).astype(jnp.float32) * (d ** -0.5)
    i_pos = np.arange(CHUNK)[:, None]
    p_pos = np.arange(BAND * CHUNK)[None, :]
    dist = LEFT_CHUNKS * CHUNK + i_pos - p_pos
    rel_idx = np.clip(dist, -(CHUNK - 1), REL_CLIP) + (CHUNK - 1)
    bias = rel_table.astype(jnp.float32)[:, rel_idx]
    scores = scores + bias[None, :, None]
    valid = jnp.repeat(band_idx >= LEFT_CHUNKS, CHUNK, axis=1)
    scores = jnp.where(valid[None, None, :, None, :], scores, NEG_BIG)
    probs = jax.nn.softmax(scores, axis=-1)
    out = jnp.einsum('bhcip,bhcpd->bhcid', probs.astype(v.dtype), vband)
    return out.reshape(b, h, seq, d)

def second_inputs(seed: int = 0) -> dict:
    key = jax.random.key(seed)
    ks = jax.random.split(key, 8)
    x = jax.random.normal(ks[0], (BATCH, SEQ, D_MODEL), jnp.float32)
    norm_g = 1.0 + 0.02 * jax.random.normal(ks[1], (DEPTH_2, D_MODEL), jnp.float32)
    w_in = jax.random.normal(ks[2], (DEPTH_2, D_MODEL, D_IN), jnp.float32) * D_MODEL ** -0.5
    q_norm_g = 1.0 + 0.02 * jax.random.normal(ks[3], (DEPTH_2, HEAD_DIM), jnp.float32)
    k_norm_g = 1.0 + 0.02 * jax.random.normal(ks[4], (DEPTH_2, HEAD_DIM), jnp.float32)
    rel_bias = 0.1 * jax.random.normal(ks[5], (DEPTH_2, N_HEADS_CH, N_REL), jnp.float32)
    w_out = jax.random.normal(ks[6], (DEPTH_2, D_MIX, D_MODEL), jnp.float32) * D_MIX ** -0.5
    return {"x": x, "norm_g": norm_g, "w_in": w_in, "q_norm_g": q_norm_g,
            "k_norm_g": k_norm_g, "rel_bias": rel_bias, "w_out": w_out}

def second_block(x, norm_g, w_in, q_norm_g, k_norm_g, rel_bias, w_out):
    splits = np.cumsum([D_SB, D_SB, D_SB, D_SB, D_CH, D_CH, D_CH])
    for layer in range(DEPTH_2):
        h = rms_norm_2(x, norm_g[layer])
        proj = jnp.einsum('bsd,de->bse', h, w_in[layer])
        qa, ka, va, ga, qb, kb, vb, gb = jnp.split(proj, splits, axis=-1)
        ya = stick_breaking_attention(split_heads(qa, N_HEADS_SB),
                                      split_heads(ka, N_HEADS_SB),
                                      split_heads(va, N_HEADS_SB))
        yb = chunk_band_attention(split_heads(qb, N_HEADS_CH),
                                  split_heads(kb, N_HEADS_CH),
                                  split_heads(vb, N_HEADS_CH),
                                  q_norm_g[layer], k_norm_g[layer], rel_bias[layer])
        mixed = jnp.concatenate([merge_heads(ya) * jax.nn.silu(ga),
                                 merge_heads(yb) * jax.nn.silu(gb)], axis=-1)
        x = x + jnp.einsum('bse,ed->bsd', mixed, w_out[layer])
    return x


def setup_inputs(seed=0):
    out = dict(first_inputs(seed))
    for name, value in second_inputs(seed + 1).items():
        if name != "x":
            out[name + "_2"] = value
    return out


def reference(
    x, c, ctx, c_ctx, ada_w, ada_b, norm_g, na_ssd_w_in, ssd_conv_w, ssd_conv_b, ssd_a_log,
    ssd_dt_bias, ssd_d, ssd_norm_g, q_norm_g, k_norm_g, na_rpb, na_ssd_w_out, sc_w_in,
    sc_conv_w, sc_w_out, norm_g_2, w_in_2, q_norm_g_2, k_norm_g_2, rel_bias_2, w_out_2,
):
    x = first_block(
        x, c, ctx, c_ctx, ada_w, ada_b, norm_g, na_ssd_w_in, ssd_conv_w, ssd_conv_b, ssd_a_log,
        ssd_dt_bias, ssd_d, ssd_norm_g, q_norm_g, k_norm_g, na_rpb, na_ssd_w_out, sc_w_in,
        sc_conv_w, sc_w_out,
    )
    return second_block(
        x, norm_g_2, w_in_2, q_norm_g_2, k_norm_g_2, rel_bias_2, w_out_2,
    )


_drawn_inputs = setup_inputs


def setup_inputs(seed=0):
    import zlib

    import numpy as np

    out = dict(_drawn_inputs(seed))
    spreads = {}
    factors = {'ctx': 2.874,
     'ssd_conv_b': 7.522,
     'ssd_d': 7.229,
     'ssd_norm_g': 4.451,
     'q_norm_g': 8.0,
     'k_norm_g': 8.0,
     'na_rpb': 8.0,
     'norm_g_2': 6.776,
     'q_norm_g_2': 8.0,
     'k_norm_g_2': 8.0,
     'rel_bias_2': 8.0}
    for name, (base, spread) in spreads.items():
        noise = np.random.default_rng([zlib.crc32(name.encode()), seed]).standard_normal(out[name].shape)
        drawn = base * np.exp(spread * noise) if base else spread * noise
        out[name] = jnp.asarray(drawn.astype(out[name].dtype))
    for name, factor in factors.items():
        out[name] = (out[name] * factor).astype(out[name].dtype)
    return out
```

```python
from contextlib import ExitStack

import concourse.bass as bass
import numpy as np
from concourse import mybir

F32 = mybir.dt.float32
ALU = mybir.AluOpType
ACT = mybir.ActivationFunctionType
AX = mybir.AxisListType
ds = bass.ds

P = 128
D = 2048
DC = D // P
T = 256
TC = 256
TB = T // P
EPS = 1e-6
BIG = 1e30
TILE = 256
SLOTS = 4
COL_Q, COL_GATE, COL_Z, COL_K, COL_V, COL_X = (n * D for n in range(6))
COL_B, COL_C = COL_X + 2048, COL_X + 3072
COL_DT = COL_X + 4096
NA_ROWS, NA_COLS = 4, 64
RPB_H, RPB_R = 15 * 31, 31
NDT = 64
RELN = 320
ATT = float(P) ** -0.5

PARAMS = [
    ("ada_b0", 48), ("ada_b1", 48), ("c", 16), ("c_ctx", 16),
    ("norm_g0", 16), ("norm_g1", 16), ("norm_g_2", 16), ("ssd_norm_g", 16), ("conv_b", 32),
    ("q_g", 1), ("k_g", 1), ("q_g2", 1), ("k_g2", 1), ("fill", 28),
    ("conv_w0", 32), ("conv_w1", 32), ("conv_w2", 32), ("conv_w3", 32),
    ("conv_w4", 32), ("sc_conv_w", 48), ("fill2", 48),
]
COLUMN = {}
_at = 0
for _name, _n in PARAMS:
    COLUMN[_name] = _at
    _at += _n
assert _at == 4 * P

CONSTS = {}
_at = 0
for _name, _n in [("ident", P), ("anti", P), ("ones", P), ("le", P), ("ge", P), ("lt", P), ("gt", P),
                  ("big_ge", P), ("na_mask", NA_COLS)]:
    CONSTS[_name] = (_at, _n)
    _at += _n
N_CONSTS = _at


def constants():
    p, f = np.arange(P)[:, None], np.arange(P)[None, :]
    one = lambda x: (x + np.zeros((P, P))).astype(np.float32)
    q, k = (P - 1 - p) % NA_COLS, np.arange(NA_COLS)[None, :]
    start = np.clip(q - 8, 0, NA_COLS - 16)
    window = np.where((k >= start) & (k < start + 16), 0.0, -BIG)
    parts = [one(p == f), one(p == P - 1 - f), one(p > -1), one(p <= f), one(p >= f), one(p < f), one(p > f),
             one(p >= f) * BIG, window]
    return np.ascontiguousarray(np.concatenate(parts, axis=1).astype(np.float32))


def wait(eng, sem, value):
    if not (isinstance(value, int) and value <= 0):
        eng.wait_ge(sem, value)


class Chain:

    def __init__(self, eng, sem, base, steps):
        self.eng, self.sem, self.base, self.steps, self.n = eng, sem, base, steps, 0

    def link(self, ins):
        ins.then_inc(self.sem, 1)
        self.n += 1
        self.eng.wait_ge(self.sem, self.base + self.n)

    def close(self):
        assert self.n == self.steps, f"{self.sem}: {self.n} links, not {self.steps}"


def iterations(eng, n, body, peeled=2):
    for i in range(peeled):
        body(i)
    if n > peeled:
        with eng.Fori(peeled, n) as i:
            body(i)


def is_first(i):
    return isinstance(i, int) and i == 0


def build(nc, ins, out, scratch):
    with ExitStack() as ctx:
        program(nc, ctx, ins, out, scratch)


def program(nc, ctx, ins, out, scratch):
    def sb(name, *shape):
        return ctx.enter_context(nc.sbuf_tensor(name, [P, *shape], F32))

    def sem(name):
        return ctx.enter_context(nc.semaphore(name))

    w = [sb(f"w{s}", DC, TILE) for s in range(SLOTS)]
    cst = sb("cst", N_CONSTS)
    hT = sb("hT", DC, T + TC)
    xT = sb("xT", DC, T)
    yT = sb("yT", 2 * DC, T)
    cxT = yT[:, DC:2 * DC, :]
    colp = sb("colp", 4 * P)
    mod = sb("mod", 2, 48, 2)
    amp = sb("amp", 3, DC)
    rs = sb("rs", T + TC)
    ssq = sb("ssq", T + TC)
    WORK = 13300
    work = sb("work", WORK)
    w3 = w[3][:, :, :].rearrange("p a b -> p (a b)")

    class Lay:

        def __init__(self, region, size):
            self.region, self.size, self.at = region, size, 0

        def __call__(self, *shape):
            n = int(np.prod(shape))
            v = self.region[:, self.at:self.at + n]
            self.at += n
            assert self.at <= self.size, self.at
            names = "abcd"[:len(shape)]
            if len(shape) > 1:
                v = v.rearrange(f"p ({' '.join(names)}) -> p {' '.join(names)}", **dict(zip(names[:-1], shape[:-1])))
            return v

    bank = [ctx.enter_context(nc.psum_tensor(f"bank{i}", [P, 512], F32)) for i in range(6)]
    wide = ctx.enter_context(nc.psum_tensor("wide", [P, 1024], F32))

    def const(name):
        a, n = CONSTS[name]
        return cst[:, a:a + n]

    def col(name, i=0):
        return colp[:, ds(COLUMN[name] + i, 1)]

    IDENT, ANTI, ONES, BIG_GE = const("ident"), const("anti"), const("ones"), const("big_ge")
    LE, GE, LT, GT = const("le"), const("ge"), const("lt"), const("gt")

    def chunk(t, c):
        return t[:, ds(c, 1), :].rearrange("p a b -> p (a b)")

    def both_diagonals(ap):
        return ap.rearrange("p (a b) -> p a b", a=4)[:, 0:4:3, :]

    L = Lay(work, WORK)
    prm = L(4, P)
    sil, sil_e = L(32), L(32)
    xrow = L(4, D)
    arow = L(2, TILE)
    L = Lay(work, WORK)
    qraw, qsq, qhat = L(2, T), L(2, T), L(2, T)
    kraw, ksq, khat = L(2, T + TC), L(2, T + TC), L(2, T + TC)
    rsn = L(3, T + TC)
    graw, gexp, gsil = L(2, T), L(2, T), L(2, T)
    vtok = L(4, TILE)
    prob = L(2, T + TC)
    probT = L(4, T)
    hankel = L(2, 6, NA_COLS)
    neg_max, row_sum, row_inv = L(2), L(2), L(2)
    qg = L(1)
    L = Lay(work, WORK)
    pad = L(2, 2, T + 4)
    acc, cexp = L(2, T + TC), L(2, T + TC)
    xc = L(2, T + TC)
    bT, cmT = L(T + TC), L(T)
    xtk = L(4, TILE)
    btk = L(2, P)
    dA, cs, ecs, toend = L(4, NDT), L(2, NDT), L(2, NDT), L(2, NDT)
    dt, dtabs = L(4, NDT), L(4, NDT)
    dbias, aneg, dskip = L(NDT), L(NDT), L(32)
    csb = L(2, 4, T)
    zraw, zexp = L(2, TILE), L(2, TILE)
    csrow = zraw.rearrange("p a b -> p (a b)")[0:NDT, 0:T]
    ssz, rz = L(2), L(2)
    cbf, cbb = L(2, P), L(2, P)
    hst = L(4 * P)
    ysd = L(2, 2, TILE)
    yz = L(2, TILE)
    L = Lay(w3, DC * TILE)
    wdt = L(DC, NDT)
    L.at = 0
    decay = L(2, 2, 3 * P)
    wm = L(2, 2 * T)
    wtmp = L(2, P)
    xe = L(2, 2, TILE)
    L = Lay(work, WORK)
    u_b, u_c, u_h, u_g, u_e = (L(2, T) for _ in range(5))
    u_pad = L(2, T + 2)
    u_out = L(2, T)
    L = Lay(work, WORK)
    q2raw, k2raw, q2, k2, k2neg = (L(2, T) for _ in range(5))
    q2sq, k2sq = L(2, T), L(2, T)
    rs2 = L(2, 2 * T)
    g2raw, g2exp, g2sil = L(2, T), L(2, T), L(2, T)
    v2 = L(2, TILE)
    zabs, zlog, stay, prob2 = (L(3 * P) for _ in range(4))
    prob2T = L(3 * P)
    hank2 = L(2, T)
    negmax2, rowsum2, rowinv2 = L(2), L(2), L(2)
    qg2 = L(1)
    o_row = L(2, TILE)
    o_col = L(2, 2, T)

    w_in = ins["na_ssd_w_in"][0].rearrange("(c p) n -> p c n", p=P)
    w_out = ins["na_ssd_w_out"][0].rearrange("(h c p) n -> h p c n", p=P, h=2)
    w_ada = [ins["ada_w"][n].rearrange("(c p) n -> p c n", p=P) for n in range(2)]
    w_sc = ins["sc_w_in"][0].rearrange("(c p) n -> p c n", p=P)
    w_sco = ins["sc_w_out"][0].rearrange("(c p) n -> p c n", p=P)
    w_in2 = ins["w_in_2"][0].rearrange("(c p) n -> p c n", p=P)
    w_out2 = ins["w_out_2"][0].rearrange("(c p) n -> p c n", p=P)

    PHASES = [("na", 8, 6, [1, 2, 4, 6]), ("ssd", 8, 6, [2, 4, 6, 6]), ("out", 4, 2, [1, 1, 2, 2]),
              ("sc", 8, 4, [1, 2, 3, 4]), ("sco", 2, 4, [1, 2, 3, 4]), ("sb", 4, 4, [1, 2, 3, 4]),
              ("ch", 4, 4, [1, 2, 3, 4]), ("out2", 2, 4, [1, 2, 3, 4])]
    ADA_IT = 6
    BANKS, GROUPS, EARLIER = {}, {}, {}
    b, g, before = 0, 2 * ADA_IT, None
    for ph in PHASES:
        BANKS[ph[0]], GROUPS[ph[0]], EARLIER[ph[0]] = b, g, before
        b, g, before = b + ph[1] * ph[2], g + ph[1], ph
    PHASE = {ph[0]: ph for ph in PHASES}

    acc_full, acc_free = sem("acc_full"), sem("acc_free")
    w_loaded = [sem(f"w_loaded{s}") for s in range(SLOTS)]
    ada_used, ada_row, ada_turned = sem("ada_used"), sem("ada_row"), sem("ada_turned")
    consts_in, params_zeroed, params_in, x_in, ssd_in = (
        sem(n) for n in ("consts_in", "params_zeroed", "params_in", "x_in", "ssd_in"))
    cols_pe, cols_dve, c_exp, c_silu, ada_full, mod_ready = (
        sem(n) for n in ("cols_pe", "cols_dve", "c_exp", "c_silu", "ada_full", "mod_ready"))
    xt_pe, xt_dve = sem("xt_pe"), sem("xt_dve")
    norm_sq, norm_sum, norm_mm, norm_rs, norm_mul, norm_out = (
        sem(f"norm_{n}") for n in ("sq", "sum", "mm", "rs", "mul", "out"))
    act_link, dve_link, ssd_sq, ssd_ln, sb_e = (sem(n) for n in ("act_link", "dve_link", "ssd_sq", "ssd_ln", "sb_e"))

    def names(prefix, *which):
        return [sem(f"{prefix}_{n}") for n in which]

    (na_ss, na_rs, na_lnfree, na_kq, na_hk_in, na_hk, na_sc, na_max, na_p, na_pn, na_pt, na_pts, na_po, na_y,
     na_g) = names("na", "ss", "rs", "lnfree", "kq", "hk_in", "hk", "sc", "max", "p", "pn", "pt", "pts", "po", "y", "g")
    (d_full, d_x, d_abs, d_log, d_a, d_cs, d_csout, d_rows, d_rowsb, d_store, d_toend, csb_in) = names(
        "dt", "full", "x", "abs", "log", "a", "cs", "csout", "rows", "rowsb", "store", "toend", "csb_in")
    (s_conv, s_exp, s_silu, s_pads, s_xt, s_xtk, s_xe, s_cb, s_st, s_h, s_dd, s_ed, s_wm, s_yi, s_ys, s_t1, s_yz,
     s_rz, s_yn, s_ft, s_y) = names("ssd", "conv", "exp", "silu", "pads", "xt", "xtk", "xe", "cb", "st", "h", "dd",
                                    "ed", "wm", "yi", "ys", "t1", "yz", "rz", "yn", "ft", "y")
    sc_y = sem("sc_y")
    (sb_kq, sb_z, sb_abs, sb_log, sb_stay, sb_w, sb_p, sb_po, sb_y, sb_g) = names(
        "sb", "kq", "z", "abs", "log", "stay", "w", "p", "po", "y", "g")
    (ch_ss, ch_rs, ch_lnfree, ch_kq, ch_hk_in, ch_mask, ch_sc, ch_max, ch_p, ch_pn, ch_pt, ch_pts, ch_po, ch_y,
     ch_g) = names("ch", "ss", "rs", "lnfree", "kq", "hk_in", "mask", "sc", "max", "p", "pn", "pt", "pts", "po", "y",
                   "g")
    o_tr, o_rows, o_out = names("o", "tr", "rows", "out")

    block = ctx.enter_context(nc.Block())

    @block.sync
    def _(sp):
        sp.dma_start(cst[:, :], ins["consts"]).then_inc(consts_in, 16)

        def load(s, src):
            sp.dma_start(w[s][:, :, 0:src.shape[2]], src).then_inc(w_loaded[s], 16)

        def columns(i, start):
            return start + i * TILE if isinstance(i, int) else sp.snap(i * TILE + start)

        for s in range(SLOTS):
            load(s, w_ada[0][:, :, s * TILE:(s + 1) * TILE])
        for layer in range(2):
            with sp.Fori(1 - layer, ADA_IT) as i:
                for s in range(SLOTS):
                    at = sp.snap(i * (SLOTS * TILE) + s * TILE)
                    sp.wait_ge(ada_used, (i + layer * ADA_IT - 1) * SLOTS + s + 1)
                    load(s, w_ada[layer][:, :, ds(at, TILE)])

        def slot_free(phase, i, s):
            if isinstance(i, int) and i == 0:
                prev = EARLIER[phase]
                if prev is None:
                    return sp.wait_ge(ada_used, (2 * ADA_IT - 1) * SLOTS + s + 1)
                name, n, per, used = prev
                return sp.wait_ge(acc_full, BANKS[name] + (n - 1) * per + used[s])
            _, _, per, used = PHASE[phase]
            sp.wait_ge(acc_full, BANKS[phase] + (i - 1) * per + used[s])

        def na_biases(a):
            at = a * (2 * 465) if isinstance(a, int) else sp.snap(a * (2 * 465))
            wait(sp, na_sc, 4 * a)
            for h in range(2):
                for half in range(2):
                    src = bass.AP(ins["na_rpb"].tensor, at + h * 465 + (5 - (1 - half)) * 31 - 48,
                                  [[1, NA_COLS], [31, 6], [1, NA_COLS]])
                    sp.dma_start(hankel[half * 64:half * 64 + 64, h, :, :], src).then_inc(na_hk_in, 16)

        def na(i):
            at = [columns(i, c) for c in (COL_Q, COL_GATE, COL_K, COL_V)]
            for s in range(SLOTS):
                slot_free("na", i, s)
                load(s, w_in[:, :, ds(at[s], TILE)])
                if s == 1 and not is_first(i):
                    na_biases(i - 1)

        iterations(sp, 8, na)

        def ssd(i):
            at = [columns(i, COL_X), columns(i, COL_Z)]
            half = [COL_B + i * P, COL_C + i * P] if isinstance(i, int) else [
                sp.snap(i * P + COL_B), sp.snap(i * P + COL_C)]
            slot_free("ssd", i, 0)
            load(0, w_in[:, :, ds(at[0], TILE)])
            slot_free("ssd", i, 1)
            for n in range(2):
                sp.dma_start(w[1][:, :, n * P:(n + 1) * P], w_in[:, :, ds(half[n], P)]).then_inc(w_loaded[1], 16)
            if is_first(i):
                na_biases(7)
            slot_free("ssd", i, 2)
            load(2, w_in[:, :, ds(at[1], TILE)])

        iterations(sp, 8, ssd)

        def out_proj(i):
            at = [sp.snap(i * (2 * TILE) + n * TILE) if not isinstance(i, int) else (2 * i + n) * TILE for n in range(2)]
            for s in range(SLOTS):
                if is_first(i) and s == 3:
                    sp.wait_ge(s_y, 16)
                else:
                    slot_free("out", i, s)
                load(s, w_out[s % 2][:, :, ds(at[s // 2], TILE)])

        iterations(sp, 4, out_proj)

        def four(phase, src, starts, step, n):
            def body(i):
                at = [c + i * step if isinstance(i, int) else sp.snap(i * step + c) for c in starts]
                for s in range(SLOTS):
                    slot_free(phase, i, s)
                    load(s, src[:, :, ds(at[s], TILE)])
                    if phase == "out2" and s == 1 and is_first(i):
                        ch_biases(3)
            iterations(sp, n, body)

        def ch_biases(a):
            at = a * (2 * RELN) if isinstance(a, int) else sp.snap(a * (2 * RELN))
            sp.wait_ge(ch_mask, 1)
            wait(sp, ch_sc, 4 * a)
            for h in range(2):
                for half, n in ((0, T), (1, T - 64)):
                    src = bass.AP(ins["rel_rev"].tensor, at + h * RELN + 1 + half * 64, [[1, 64], [1, n]])
                    sp.dma_start(hank2[half * 64:half * 64 + 64, h, 0:n], src).then_inc(ch_hk_in, 16)

        four("sc", w_sc, [n * D for n in range(4)], TILE, 8)
        four("sco", w_sco, [n * TILE for n in range(4)], 4 * TILE, 2)
        four("sb", w_in2, [n * 1024 for n in (0, 1, 3, 2)], TILE, 4)

        def ch(i):
            at = [4096 + n * 1024 + i * TILE if isinstance(i, int) else sp.snap(i * TILE + (4096 + n * 1024))
                  for n in (0, 1, 3, 2)]
            for s in range(SLOTS):
                slot_free("ch", i, s)
                load(s, w_in2[:, :, ds(at[s], TILE)])
                if s == 1 and not is_first(i):
                    ch_biases(i - 1)

        iterations(sp, 4, ch)
        four("out2", w_out2, [n * TILE for n in range(4)], 4 * TILE, 2)

    @block.tensor
    def _(pe):
        def mm(dst, lhsT, rhs, start=True, stop=True, free=False):
            return nc.tensor.matmul(dst, lhsT, rhs, start=start, stop=stop, skip_group_check=free)

        def tr(dst, src, n=P):
            return nc.tensor.transpose(dst, src, IDENT[0:n, 0:n])

        def loaded(s, phase, i):
            g = GROUPS[phase]
            extra = 0
            if s == 1:
                extra = 16 * (i + 1) if phase == "ssd" else (16 * 8 if g > GROUPS["ssd"] else 0)
            if s == 3 and g > GROUPS["ssd"]:
                extra = -16 * 8
            pe.wait_ge(w_loaded[s], 16 * (g + 1) + 16 * i + extra)

        def accumulate(phase, n, i):
            k = BANKS[phase] + i * PHASE[phase][2] + n
            wait(pe, acc_free, k - 1)
            return bank[n % 2]

        def featured(dst, s, ch, width, ready=None):
            for kc in range(DC):
                if ready:
                    pe.wait_ge(norm_out, ready(kc))
                last = mm(dst, w[s][:, kc, ch * P:(ch + 1) * P], hT[:, kc, 0:width], kc == 0, kc == DC - 1)
            return last

        def tokened(dst, s, tb, width=TILE, weights=None):
            src = w[s] if weights is None else weights
            for kc in range(DC):
                last = mm(dst, hT[:, kc, tb * P:(tb + 1) * P], src[:, kc, 0:width], kc == 0, kc == DC - 1)
            return last

        pe.wait_ge(consts_in, 16)
        pe.wait_ge(params_in, 16 * 21)
        for n in range(4):
            last = tr(bank[2][:, n * P:(n + 1) * P], prm[:, n, :])
        last.then_inc(cols_pe, 1)
        pe.wait_ge(x_in, 64)
        for kc in range(DC):
            if kc >= 3:
                pe.wait_ge(xt_dve, kc - 2)
            for tb in range(4):
                last = tr(bank[3 + kc % 3][:, tb * P:(tb + 1) * P], xrow[:, tb, kc * P:(kc + 1) * P])
            last.then_inc(xt_pe, 1)
        pe.wait_ge(c_silu, 1)
        pe.wait_ge(xt_dve, DC)
        pair = sil.rearrange("p (a b) -> p b a", a=2)
        for layer in range(2):
            def ada(i, layer=layer):
                t = i * SLOTS + layer * ADA_IT * SLOTS

                def turn(s):
                    pe.wait_ge(ada_row, t + s + 1)
                    for ch in range(2):
                        last = mm(bank[layer][:, ds(i * 16 + s * 4 + ch * 2, 2)], arow[0:2, s % 2, ch * P:(ch + 1) * P],
                                  IDENT[0:2, 0:2])
                    last.then_inc(ada_turned, 1)

                for s in range(SLOTS):
                    pe.wait_ge(w_loaded[s], 16 * (i + layer * ADA_IT + 1))
                    wait(pe, ada_row, t + s - 1)
                    for kc in range(DC):
                        last = mm(bank[3 + s % 2][0:2, 0:TILE], pair[:, kc, :], w[s][:, kc, :], kc == 0, kc == DC - 1)
                    last.then_inc(ada_used, 1)
                    if s:
                        turn(s - 1)
                turn(SLOTS - 1)

            iterations(pe, ADA_IT, ada, 1)

        def norm_sums(n, width):
            pe.wait_ge(norm_sum, n + 1)
            mm(bank[2][:, 0:width], ONES, ssq[:, 0:width]).then_inc(norm_mm, 1)

        norm_sums(0, T + TC)

        def na_scores(a, h):
            pe.wait_ge(na_kq, 3 * a + 3)
            pe.wait_ge(na_hk, a + 1)
            wait(pe, na_p, 4 * a + 2 * h)
            for qb in range(2):
                mm(bank[3 + qb][:, :], qhat[:, h, qb * P:(qb + 1) * P], khat[:, h, :], True, False)
                rows = hankel[:, h, 2 - 2 * qb:6 - 2 * qb, :].rearrange("p a b -> p (a b)")
                mm(bank[3 + qb][:, 0:T], ANTI, rows, False, True).then_inc(na_sc, 1)

        def na_transposes(a, h):
            pe.wait_ge(na_pn, 4 * a + 2 * h + 2)
            wait(pe, na_pts, 2 * a + h)
            for kb in range(4):
                for qb in range(2):
                    last = tr(wide[:, kb * T + qb * P:kb * T + (qb + 1) * P], prob[:, qb, kb * P:(kb + 1) * P])
            last.then_inc(na_pt, 1)

        def na_values(a, h):
            pe.wait_ge(na_pts, 2 * a + h + 1)
            pe.wait_ge(acc_free, BANKS["na"] + 6 * a + 6)
            wait(pe, na_y, 2 * a + h)
            for kb in range(4):
                last = mm(bank[5][:, 0:T], vtok[:, kb, h * P:(h + 1) * P], probT[:, kb, :], kb == 0, kb == 3)
            last.then_inc(na_po, 1)

        def na(i):
            first = is_first(i)
            a = i - 1
            loaded(0, "na", i)
            dst = accumulate("na", 0, i)
            for ch in range(2):
                last = featured(dst[:, ch * T:(ch + 1) * T], 0, ch, T, (lambda kc: 2 * kc + 1) if first and ch == 0 else None)
            last.then_inc(acc_full, 1)
            if not first:
                na_scores(a, 0)
            loaded(1, "na", i)
            dst = accumulate("na", 1, i)
            for ch in range(2):
                last = featured(dst[:, ch * T:(ch + 1) * T], 1, ch, T)
            last.then_inc(acc_full, 1)
            if not first:
                na_transposes(a, 0)
                na_scores(a, 1)
            pe.wait_ge(acc_free, BANKS["na"] + 6 * i + 1)
            wait(pe, na_lnfree, 3 * i)
            mm(bank[2][:, :], ONES, qsq.rearrange("p a b -> p (a b)")).then_inc(na_ss, 1)
            loaded(2, "na", i)
            for ch in range(2):
                dst = accumulate("na", 2 + ch, i)
                if first:
                    pe.wait_ge(norm_out, 2 * DC)
                featured(dst[:, :], 2, ch, T + TC).then_inc(acc_full, 1)
                if not first and ch == 0:
                    na_values(a, 0)
                    na_transposes(a, 1)
            if not first:
                na_values(a, 1)
            loaded(3, "na", i)
            for half in range(2):
                pe.wait_ge(acc_free, BANKS["na"] + 6 * i + 3 + half)
                pe.wait_ge(na_lnfree, 3 * i + 1 + half)
                mm(bank[2][:, :], ONES, ksq[:, half, :]).then_inc(na_ss, 1)
                dst = accumulate("na", 4 + half, i)
                for tb in range(2):
                    last = tokened(dst[:, tb * TILE:(tb + 1) * TILE], 3, 2 * half + tb)
                last.then_inc(acc_full, 1)

        iterations(pe, 8, na)
        for h in range(2):
            na_scores(7, h)
            na_transposes(7, h)
            na_values(7, h)

        def steps_of_dt():
            pe.wait_ge(ssd_in, 64)
            for tb in range(4):
                last = tokened(bank[2][:, tb * NDT:(tb + 1) * NDT], 0, tb, NDT, wdt)
            last.then_inc(d_full, 1)

        def sums_of_dt():
            pe.wait_ge(d_a, 1)
            F, B = slice(0, 32), slice(32, 64)
            fwd, bwd = lambda tb: dA[:, tb, F], lambda tb: dA[:, tb, B]
            o = bank[3]
            mm(o[:, 0:32], LE, fwd(0))
            mm(o[:, 64:96], LE, fwd(1), True, False)
            mm(o[:, 64:96], ONES, fwd(0), False, True)
            mm(o[:, 96:128], GE, bwd(1))
            mm(o[:, 32:64], GE, bwd(0), True, False)
            mm(o[:, 32:64], ONES, bwd(1), False, True)
            mm(o[:, 192:224], GT, fwd(3))
            mm(o[:, 128:160], GT, fwd(2), True, False)
            mm(o[:, 128:160], ONES, fwd(3), False, True)
            mm(o[:, 160:192], LT, bwd(2))
            mm(o[:, 224:256], LT, bwd(3), True, False)
            mm(o[:, 224:256], ONES, bwd(2), False, True).then_inc(d_cs, 1)
            pe.wait_ge(d_csout, 3)
            for tb in range(2):
                last = tr(bank[4][0:NDT, tb * P:(tb + 1) * P], cs[:, tb, :])
            last.then_inc(d_rows, 1)

        def ssd(g):
            first = is_first(g)
            s = g - 1
            loaded(0, "ssd", g)
            dst = accumulate("ssd", 0, g)
            featured(dst[:, :], 0, 0, T + TC).then_inc(acc_full, 1)
            if first:
                steps_of_dt()
            else:
                pe.wait_ge(s_xtk, g)
                pe.wait_ge(s_silu, 4 * g)
                for jb in range(2):
                    last = mm(bank[2][:, jb * T:(jb + 1) * T], bT[:, jb * P:(jb + 1) * P], cmT[:, :])
                last.then_inc(s_cb, 1)
            dst = accumulate("ssd", 1, g)
            featured(dst[:, :], 0, 1, T + TC).then_inc(acc_full, 1)
            if first:
                sums_of_dt()
            else:
                pe.wait_ge(s_xe, g)
                wait(pe, s_y, 2 * s)
                for d in range(2):
                    for jb in range(2):
                        last = mm(bank[3][:, d * TILE:(d + 1) * TILE], btk[:, jb, :], xe[:, d, jb, :], jb == 0, jb == 1)
                last.then_inc(s_st, 1)
                ssd_apply(s)
            loaded(1, "ssd", g)
            dst = accumulate("ssd", 2, g)
            featured(dst[:, :], 1, 0, T + TC).then_inc(acc_full, 1)
            dst = accumulate("ssd", 3, g)
            featured(dst[:, 0:T], 1, 1, T).then_inc(acc_full, 1)
            loaded(2, "ssd", g)
            for tb in range(2):
                dst = accumulate("ssd", 4 + tb, g)
                tokened(dst[:, 0:TILE], 2, tb).then_inc(acc_full, 1)
            if not first:
                ssd_features(s)
            pe.wait_ge(s_silu, 4 * g + 3)
            if not first:
                pe.wait_ge(s_t1, 2 * s + 2)
            for tb in range(4):
                for c in range(2):
                    tr(wide[:, tb * TILE + c * P:tb * TILE + (c + 1) * P], xc[:, c, tb * P:(tb + 1) * P])
            for jb in range(2):
                last = tr(bank[5][:, jb * P:(jb + 1) * P], bT[:, T + jb * P:T + (jb + 1) * P])
            last.then_inc(s_xt, 1)

        def ssd_apply(s):
            pe.wait_ge(s_h, s + 1)
            pe.wait_ge(s_xtk, s + 1)
            for ib, dst in enumerate((bank[5][:, :], wide[:, 0:512])):
                last = mm(dst, cmT[:, ib * P:(ib + 1) * P], hst)
            last.then_inc(s_ys, 1)
            wait(pe, s_yz, 1 * s)
            for r in range(4):
                pe.wait_ge(s_wm, 4 * s + r + 1)
                for ib in range(2):
                    o = ib * TILE + r * 64
                    for jb in range(2):
                        last = mm(bank[4][:, o:o + 64], wm[:, r % 2, jb * T + ib * P:jb * T + (ib + 1) * P],
                                  xtk[:, jb, r * 64:(r + 1) * 64], jb == 0, jb == 1)
                last.then_inc(s_yi, 1)

        def ssd_features(s):
            pe.wait_ge(s_yn, 2 * s + 2)
            for c in range(2):
                for ib in range(2):
                    last = tr(bank[3][:, c * T + ib * P:c * T + (ib + 1) * P], yz[:, ib, c * P:(c + 1) * P])
            last.then_inc(s_ft, 1)

        iterations(pe, 8, ssd)
        pe.wait_ge(s_xtk, 8)
        pe.wait_ge(s_silu, 32)
        for jb in range(2):
            last = mm(bank[2][:, jb * T:(jb + 1) * T], bT[:, jb * P:(jb + 1) * P], cmT[:, :])
        last.then_inc(s_cb, 1)
        pe.wait_ge(s_xe, 8)
        pe.wait_ge(s_y, 14)
        for d in range(2):
            for jb in range(2):
                last = mm(bank[3][:, d * TILE:(d + 1) * TILE], btk[:, jb, :], xe[:, d, jb, :], jb == 0, jb == 1)
        last.then_inc(s_st, 1)
        ssd_apply(7)
        ssd_features(7)

        pe.wait_ge(s_y, 16)

        def out_proj(i):
            for cb in range(2):
                loaded(2 * cb, "out", i)
                loaded(2 * cb + 1, "out", i)
                dst = accumulate("out", cb, i)
                for ch in range(2):
                    for k in range(2 * DC):
                        last = mm(dst[:, ch * T:(ch + 1) * T], w[2 * cb + k // DC][:, k % DC, ch * P:(ch + 1) * P],
                                  yT[:, k, :], k == 0, k == 2 * DC - 1)
                last.then_inc(acc_full, 1)

        iterations(pe, 4, out_proj)
        norm_sums(1, T)

        def sc(i):
            for s in range(SLOTS):
                loaded(s, "sc", i)
                dst = accumulate("sc", s, i)
                for ch in range(2):
                    last = featured(dst[:, ch * T:(ch + 1) * T], s, ch, T,
                                    (lambda kc: 2 * DC + kc + 1) if is_first(i) and s + ch == 0 else None)
                last.then_inc(acc_full, 1)

        iterations(pe, 8, sc)
        pe.wait_ge(sc_y, 16)

        def out_short(phase, n):
            def body(i):
                for s in range(SLOTS):
                    loaded(s, phase, i)
                    dst = accumulate(phase, s, i)
                    for ch in range(2):
                        for kc in range(DC):
                            last = mm(dst[:, ch * T:(ch + 1) * T], w[s][:, kc, ch * P:(ch + 1) * P], yT[:, kc, :],
                                      kc == 0, kc == DC - 1)
                    last.then_inc(acc_full, 1)
                    if phase == "out2":
                        rows(4 * i + s - 1, s)
            iterations(pe, n, body)

        out_short("sco", 2)
        norm_sums(2, T)

        def sb_scores(a, h):
            pe.wait_ge(sb_kq, 2 * a + 2)
            wait(pe, sb_stay, 2 * a + h)
            mm(bank[3][:, 0:T], k2[:, h, 0:P], q2[:, h, :])
            mm(bank[3][:, T:T + P], k2[:, h, P:T], q2[:, h, P:T]).then_inc(sb_z, 1)

        def sb_weights(a, h):
            pe.wait_ge(sb_stay, 2 * a + h + 1)
            wait(pe, sb_p, 2 * a + h)
            o = bank[4]
            mm(o[:, 0:T], k2neg[:, h, 0:P], q2[:, h, :], True, False, True)
            mm(o[:, T:T + P], k2neg[:, h, P:T], q2[:, h, P:T], False, False, True)
            mm(o[:, 0:T], GE, stay[:, 0:T], False, False, True)
            mm(o[:, T:T + P], GE, stay[:, T:T + P], False, False, True)
            mm(o[:, P:T], ONES, stay[:, T:T + P], False, False, True)
            mm(o[:, 0:P], IDENT, BIG_GE, False, False, True)
            mm(o[:, T:T + P], IDENT, BIG_GE, False, True, True).then_inc(sb_w, 1)

        def values2(phase, a, h, p_ready, src, po, y):
            pe.wait_ge(p_ready, 2 * a + h + 1)
            pe.wait_ge(acc_free, BANKS[phase] + 4 * a + 4)
            wait(pe, y, 2 * a + h)
            mm(bank[5][:, 0:T], v2[:, 0, h * P:(h + 1) * P], src[:, 0:T], True, False)
            mm(bank[5][:, P:T], v2[:, 1, h * P:(h + 1) * P], src[:, T:T + P], False, True).then_inc(po, 1)

        def sbreak(i):
            first = is_first(i)
            a = i - 1
            for s, todo in enumerate((lambda: sb_scores(a, 0),
                                      lambda: (sb_weights(a, 0), sb_scores(a, 1)),
                                      lambda: (values2("sb", a, 0, sb_p, prob2, sb_po, sb_y), sb_weights(a, 1),
                                               values2("sb", a, 1, sb_p, prob2, sb_po, sb_y)))):
                project2("sb", s, i, first)
                if not first:
                    todo()
            values_of("sb", i)

        def project2(phase, n, i, first):
            dst = accumulate(phase, n, i)
            loaded(n, phase, i)
            for ch in range(2):
                last = featured(dst[:, ch * T:(ch + 1) * T], n, ch, T,
                                (lambda kc: 3 * DC + kc + 1) if first and phase == "sb" and n + ch == 0 else None)
            last.then_inc(acc_full, 1)

        def values_of(phase, i):
            dst = accumulate(phase, 3, i)
            loaded(3, phase, i)
            for tb in range(2):
                last = tokened(dst[:, tb * TILE:(tb + 1) * TILE], 3, tb)
            last.then_inc(acc_full, 1)

        iterations(pe, 4, sbreak)
        for h in range(2):
            sb_scores(3, h)
            sb_weights(3, h)
            values2("sb", 3, h, sb_p, prob2, sb_po, sb_y)

        def ch_scores(a, h):
            pe.wait_ge(ch_kq, 2 * a + 2)
            pe.wait_ge(ch_hk_in, 64 * a + 64)
            wait(pe, ch_p, 4 * a + 2 * h)
            o = bank[3]
            mm(o[:, 0:P], q2[:, h, 0:P], k2[:, h, 0:P], True, False)
            mm(o[:, 0:P], ANTI, hank2[:, h, P:T], False, True).then_inc(ch_sc, 1)
            o = bank[4]
            mm(o[:, 0:T], q2[:, h, P:T], k2[:, h, :], True, False)
            mm(o[:, 0:T], ANTI, hank2[:, h, :], False, True).then_inc(ch_sc, 1)

        def ch_transposes(a, h):
            pe.wait_ge(ch_pn, 4 * a + 2 * h + 2)
            wait(pe, ch_pts, 2 * a + h)
            for n in range(3):
                last = tr(wide[:, n * P:(n + 1) * P], prob2[:, n * P:(n + 1) * P])
            last.then_inc(ch_pt, 1)

        def chband(i):
            first = is_first(i)
            a = i - 1
            project2("ch", 0, i, first)
            if not first:
                ch_scores(a, 0)
            project2("ch", 1, i, first)
            if not first:
                ch_transposes(a, 0)
                ch_scores(a, 1)
            project2("ch", 2, i, first)
            if not first:
                values2("ch", a, 0, ch_pts, prob2T, ch_po, ch_y)
                ch_transposes(a, 1)
            for n, sq in enumerate((q2sq, k2sq)):
                pe.wait_ge(acc_free, BANKS["ch"] + 4 * i + 1 + n)
                wait(pe, ch_lnfree, 2 * i + n)
                mm(bank[2][:, :], ONES, sq.rearrange("p a b -> p (a b)")).then_inc(ch_ss, 1)
            if not first:
                values2("ch", a, 1, ch_pts, prob2T, ch_po, ch_y)
            values_of("ch", i)

        iterations(pe, 4, chband)
        for h in range(2):
            ch_scores(3, h)
            ch_transposes(3, h)
            values2("ch", 3, h, ch_pts, prob2T, ch_po, ch_y)

        pe.wait_ge(ch_y, 8)

        def rows(n, s):
            if isinstance(n, int) and n < 0:
                return
            pe.wait_ge(acc_free, BANKS["out2"] + n + 1)
            wait(pe, o_rows, n)
            for tb in range(2):
                for c in range(2):
                    last = tr(wide[:, tb * TILE + c * P:tb * TILE + (c + 1) * P],
                              o_col[:, (s + 1) % 2, c, tb * P:(tb + 1) * P])
            last.then_inc(o_tr, 1)

        out_short("out2", 2)
        rows(7, 0)

    @block.scalar
    def _(act):
        def A(*args, **kw):
            return nc.scalar.activation(*args, **kw)

        act.wait_ge(params_zeroed, 1)
        rows = {"ada_b0": ins["ada_b"][0], "ada_b1": ins["ada_b"][1], "c": ins["c"][0], "c_ctx": ins["c_ctx"],
                "norm_g0": ins["norm_g"][0], "norm_g1": ins["norm_g"][1], "norm_g_2": ins["norm_g_2"][0],
                "ssd_norm_g": ins["ssd_norm_g"][0], "conv_b": ins["ssd_conv_b"][0], "q_g": ins["q_norm_g"][0],
                "k_g": ins["k_norm_g"][0], "q_g2": ins["q_norm_g_2"][0], "k_g2": ins["k_norm_g_2"][0]}
        for k in range(5):
            rows[f"conv_w{k}"] = ins["ssd_conv_w"][0, k]
        for k in range(3):
            rows[f"sc{k}"] = ins["sc_conv_w"][0, k]
        n_rows = 0
        for name, src in rows.items():
            at = COLUMN["sc_conv_w"] + 16 * int(name[2]) if name in ("sc0", "sc1", "sc2") else COLUMN[name]
            n = src.shape[0] // P
            act.dma_start(prm[at % P:at % P + n, at // P, :], src.rearrange("(a b) -> a b", b=P)).then_inc(params_in, 16)
            n_rows += 1
        assert n_rows == 21
        for src, at in ((ins["x"][0], 0), (ins["ctx"][0], 2)):
            for tb in range(2):
                act.dma_start(xrow[:, at + tb, :], src[tb * P:(tb + 1) * P, :]).then_inc(x_in, 16)
        act.wait_ge(cols_dve, 1)
        A(sil_e, colp[:, ds(COLUMN["c"], 32)], ACT.Exp, scale=-1.0).then_inc(c_exp, 1)
        links = [0]

        def link(ins_):
            links[0] += 1
            ins_.then_inc(act_link, 1)
            act.wait_ge(act_link, links[0])

        def norm(n, sources, ready):
            ready()
            for k, src in enumerate(sources):
                A(hT[:, :, k * T:(k + 1) * T], src, ACT.Square).then_inc(norm_sq, 1)
            width = T * len(sources)
            act.wait_ge(norm_mm, n + 1)
            link(A(rs[:, 0:width], bank[2][:, 0:width], ACT.Ln, scale=1.0 / D, bias=EPS))
            A(rs[:, 0:width], rs[:, 0:width], ACT.Exp, scale=-0.5).then_inc(norm_rs, 1)

        norm(0, (xT[:, :, :], cxT), lambda: act.wait_ge(xt_dve, DC))
        act.wait_ge(mod_ready, 2)
        for kc in range(DC):
            for k in range(2):
                act.wait_ge(norm_mul, 2 * kc + k + 1)
                v = hT[:, kc, k * T:(k + 1) * T]
                A(v, v, ACT.Identity, bias=mod[:, 0, kc, k:k + 1]).then_inc(norm_out, 1)

        def full(phase, n, i):
            act.wait_ge(acc_full, BANKS[phase] + i * PHASE[phase][2] + n + 1)

        def na_exp(a, h):
            wait(act, na_pt, 2 * a + h)
            for qb in range(2):
                act.wait_ge(na_max, 4 * a + 2 * h + qb + 1)
                A(prob[:, qb, :], bank[3 + qb][:, :], ACT.Exp, bias=neg_max[:, qb:qb + 1],
                  accum_out=row_sum[:, qb:qb + 1]).then_inc(na_p, 1)

        def na_rms(i, n):
            act.wait_ge(na_ss, 3 * i + n + 1)
            wait(act, na_kq, 3 * i)
            A(rsn[:, n, :], bank[2][:, :], ACT.Ln, scale=1.0 / P, bias=EPS).then_inc(na_lnfree, 1)
            act.wait_ge(na_lnfree, 3 * i + n + 1)
            A(rsn[:, n, :], rsn[:, n, :], ACT.Exp, scale=-0.5).then_inc(na_rs, 1)

        def na(i):
            first = is_first(i)
            a = i - 1
            if first:
                act.wait_ge(norm_out, 2 * DC)
            full("na", 0, i)
            wait(act, na_kq, 3 * i)
            A(qraw.rearrange("p a b -> p (a b)"), bank[0][:, :], ACT.Copy)
            wait(act, na_ss, 3 * i)
            A(qsq.rearrange("p a b -> p (a b)"), bank[0][:, :], ACT.Square).then_inc(acc_free, 1)
            if not first:
                na_exp(a, 0)
            full("na", 1, i)
            wait(act, na_g, i)
            A(graw.rearrange("p a b -> p (a b)"), bank[1][:, :], ACT.Copy)
            A(gexp.rearrange("p a b -> p (a b)"), bank[1][:, :], ACT.Exp, scale=-1.0).then_inc(acc_free, 1)
            if not first:
                na_exp(a, 1)
            na_rms(i, 0)
            for ch in range(2):
                full("na", 2 + ch, i)
                A(kraw[:, ch, :], bank[ch][:, :], ACT.Copy)
                A(ksq[:, ch, :], bank[ch][:, :], ACT.Square).then_inc(acc_free, 1)
            for half in range(2):
                na_rms(i, 1 + half)
                full("na", 4 + half, i)
                wait(act, na_po, 2 * i)
                A(vtok[:, 2 * half:2 * half + 2, :].rearrange("p a b -> p (a b)"), bank[half][:, :],
                  ACT.Copy).then_inc(acc_free, 1)

        iterations(act, 8, na)
        for h in range(2):
            na_exp(7, h)

        def ssd_setup():
            act.wait_ge(na_y, 16)
            act.dma_start(wdt, w_in[:, :, COL_DT:COL_DT + NDT]).then_inc(ssd_in, 16)
            flat = lambda a, n: bass.AP(a.tensor, a.offset, [[0, P], [1, n]])
            act.dma_start(dbias, flat(ins["ssd_dt_bias"], NDT)).then_inc(ssd_in, 16)
            act.dma_start(aneg, flat(ins["ssd_a_log"], NDT)).then_inc(ssd_in, 16)
            act.dma_start(dskip, flat(ins["ssd_d"], 32)).then_inc(ssd_in, 16)

        def ssd_dt():
            act.wait_ge(ssd_in, 64)
            link(A(aneg, aneg, ACT.Exp))
            act.wait_ge(d_abs, 1)
            f = dtabs.rearrange("p a b -> p (a b)")
            link(A(f, f, ACT.Exp, scale=-1.0))
            A(f, f, ACT.Ln, bias=1.0).then_inc(d_log, 1)
            act.wait_ge(d_cs, 1)
            flat = lambda v: v.rearrange("p a b -> p (a b)")
            A(flat(cs), bank[3][:, 0:128], ACT.Copy).then_inc(d_csout, 1)
            A(flat(ecs), bank[3][:, 0:128], ACT.Exp).then_inc(d_csout, 1)
            A(flat(toend), bank[3][:, 128:256], ACT.Exp).then_inc(d_csout, 1)
            act.wait_ge(d_rows, 1)
            A(csrow, bank[4][0:NDT, 0:T], ACT.Copy).then_inc(d_rowsb, 1)
            act.wait_ge(d_rowsb, 1)
            act.dma_start(scratch, csrow).then_inc(d_store, 16)
            act.wait_ge(d_store, 16)

        def cs_rows(s):
            at = s * (4 * T) if isinstance(s, int) else act.snap(s * (4 * T))
            wait(act, s_dd, 4 * s)
            for d in range(2):
                src = bass.AP(scratch.tensor, at + d * 32 * T, [[0, P], [T, 4], [1, T]])
                act.dma_start(csb[:, d, :, :], src).then_inc(csb_in, 16)

        def conv_in(g, n):
            full("ssd", n, g)
            wait(act, s_conv, 4 * g + n - 1)
            if is_first(g):
                act.wait_ge(s_pads, 1)
            seqs = 2 if n < 3 else 1
            A(pad[:, n % 2, 0:seqs, 2:T + 2], bank[n % 2][:, 0:seqs * T].rearrange("p (a b) -> p a b", a=seqs),
              ACT.Copy).then_inc(acc_free, 1)

        def conv_exp(g, n):
            act.wait_ge(s_conv, 4 * g + n + 1)
            wait(act, s_silu, 4 * g + n - 1)
            width = T + TC if n < 3 else T
            A(cexp[:, n % 2, 0:width], acc[:, n % 2, 0:width], ACT.Exp, scale=-1.0).then_inc(s_exp, 1)

        def ssd_states(s):
            act.wait_ge(s_st, s + 1)
            wait(act, s_ys, s)
            A(hst, bank[3][:, :], ACT.Copy).then_inc(s_h, 1)

        def ssd_scan(s):
            for r in range(4):
                act.wait_ge(s_dd, 4 * s + r + 1)
                v = decay[:, r % 2, :, :]
                A(v, v, ACT.Exp).then_inc(s_ed, 1)

        def ssd_rms(s):
            act.wait_ge(s_yz, s + 1)
            for ib in range(2):
                A(zexp[:, ib, :], yz[:, ib, :], ACT.Square, accum_out=ssz[:, ib:ib + 1]).then_inc(ssd_sq, 1)
            act.wait_ge(ssd_sq, 2 * s + 2)
            A(rz, ssz, ACT.Ln, scale=1.0 / TILE, bias=EPS).then_inc(ssd_ln, 1)
            act.wait_ge(ssd_ln, s + 1)
            A(rz, rz, ACT.Exp, scale=-0.5).then_inc(s_rz, 1)

        def ssd(g):
            first = is_first(g)
            conv_in(g, 0)
            if first:
                ssd_dt()
            else:
                ssd_scan(g - 1)
            conv_in(g, 1)
            if not first:
                ssd_states(g - 1)
            conv_exp(g, 0)
            conv_exp(g, 1)
            if not first:
                ssd_rms(g - 1)
            conv_in(g, 2)
            conv_exp(g, 2)
            conv_in(g, 3)
            conv_exp(g, 3)
            if not first:
                act.wait_ge(s_yn, 2 * g)
            for tb in range(2):
                full("ssd", 4 + tb, g)
                A(zraw[:, tb, :], bank[tb][:, 0:TILE], ACT.Copy)
                A(zexp[:, tb, :], bank[tb][:, 0:TILE], ACT.Exp, scale=-1.0).then_inc(acc_free, 1)
            cs_rows(g)

        ssd_setup()
        iterations(act, 8, ssd)
        ssd_scan(7)
        ssd_states(7)
        ssd_rms(7)

        def out_done(n):
            return lambda: act.wait_ge(acc_free, n)

        norm(1, (xT[:, :, :],), out_done(BANKS["sc"]))
        for kc in range(DC):
            act.wait_ge(norm_mul, 2 * DC + kc + 1)
            v = hT[:, kc, 0:T]
            A(v, v, ACT.Identity, bias=mod[:, 1, kc, 0:1]).then_inc(norm_out, 1)

        def sc(i):
            wait(act, sc_y, 2 * i)
            for n, dst in enumerate((u_b, u_c, u_h, u_g)):
                full("sc", n, i)
                last = A(dst.rearrange("p a b -> p (a b)"), bank[n % 2][:, :], ACT.Copy)
                if n == 3:
                    last = A(u_e.rearrange("p a b -> p (a b)"), bank[1][:, :], ACT.Exp, scale=-1.0)
                last.then_inc(acc_free, 1)

        iterations(act, 8, sc)

        norm(2, (xT[:, :, :],), out_done(BANKS["sb"]))

        def sb_logs(a, h):
            f = 2 * a + h
            act.wait_ge(sb_z, f + 1)
            wait(act, sb_stay, f)
            A(zabs, bank[3][:, 0:3 * P], ACT.Abs).then_inc(sb_abs, 1)
            act.wait_ge(sb_abs, f + 1)
            A(zabs, zabs, ACT.Exp, scale=-1.0).then_inc(sb_e, 1)
            act.wait_ge(sb_e, f + 1)
            A(zlog, zabs, ACT.Ln, bias=1.0).then_inc(sb_log, 1)

        def sb_exp(a, h):
            act.wait_ge(sb_w, 2 * a + h + 1)
            wait(act, sb_po, 2 * a + h)
            A(prob2, bank[4][:, 0:3 * P], ACT.Exp, scale=-1.0).then_inc(sb_p, 1)

        def empty2(phase, n, i, dst, func=ACT.Copy, scale=1.0, last=True):
            r = A(dst.rearrange("p a b -> p (a b)"), bank[n % 2][:, :], func, scale=scale)
            if last:
                r.then_inc(acc_free, 1)

        def sbreak(i):
            first = is_first(i)
            a = i - 1
            full("sb", 0, i)
            wait(act, sb_kq, 2 * i)
            empty2("sb", 0, i, q2raw)
            if not first:
                sb_logs(a, 0)
            full("sb", 1, i)
            empty2("sb", 1, i, k2raw)
            if not first:
                sb_exp(a, 0)
                sb_logs(a, 1)
            full("sb", 2, i)
            wait(act, sb_g, i)
            empty2("sb", 2, i, g2raw, last=False)
            empty2("sb", 2, i, g2exp, ACT.Exp, -1.0)
            if not first:
                sb_exp(a, 1)
            full("sb", 3, i)
            wait(act, sb_po, 2 * i)
            empty2("sb", 3, i, v2)

        iterations(act, 4, sbreak)
        sb_logs(3, 0)
        sb_exp(3, 0)
        sb_logs(3, 1)
        sb_exp(3, 1)

        def ch_exp(a, h):
            wait(act, ch_pt, 2 * a + h)
            for qb, (lo, hi) in enumerate(((0, P), (P, 3 * P))):
                act.wait_ge(ch_max, 4 * a + 2 * h + qb + 1)
                A(prob2[:, lo:hi], bank[3 + qb][:, 0:hi - lo], ACT.Exp, bias=negmax2[:, qb:qb + 1],
                  accum_out=rowsum2[:, qb:qb + 1]).then_inc(ch_p, 1)

        def chband(i):
            first = is_first(i)
            a = i - 1
            if first:
                act.wait_ge(sb_y, 8)
            full("ch", 0, i)
            wait(act, ch_kq, 2 * i)
            empty2("ch", 0, i, q2raw, last=False)
            empty2("ch", 0, i, q2sq, ACT.Square)
            if not first:
                ch_exp(a, 0)
            full("ch", 1, i)
            empty2("ch", 1, i, k2raw, last=False)
            empty2("ch", 1, i, k2sq, ACT.Square)
            if not first:
                ch_exp(a, 1)
            full("ch", 2, i)
            wait(act, ch_g, i)
            empty2("ch", 2, i, g2raw, last=False)
            empty2("ch", 2, i, g2exp, ACT.Exp, -1.0)
            for n in range(2):
                act.wait_ge(ch_ss, 2 * i + n + 1)
                A(rs2[:, n, :], bank[2][:, :], ACT.Ln, scale=1.0 / P, bias=EPS).then_inc(ch_lnfree, 1)
                act.wait_ge(ch_lnfree, 2 * i + n + 1)
                A(rs2[:, n, :], rs2[:, n, :], ACT.Exp, scale=-0.5).then_inc(ch_rs, 1)
            full("ch", 3, i)
            wait(act, ch_po, 2 * i)
            empty2("ch", 3, i, v2)

        iterations(act, 4, chband)
        for h in range(2):
            ch_exp(3, h)

        def rows_out(n):
            at = n * TILE if isinstance(n, int) else act.snap(n * TILE)
            act.wait_ge(o_tr, n + 1)
            wait(act, o_out, 32 * n)
            A(o_row.rearrange("p a b -> p (a b)"), wide[:, 0:2 * TILE], ACT.Copy).then_inc(o_rows, 1)
            act.wait_ge(o_rows, n + 1)
            for tb in range(2):
                act.dma_start(out[0, tb * P:(tb + 1) * P, ds(at, TILE)], o_row[:, tb, :]).then_inc(o_out, 16)

        iterations(act, 8, rows_out)
        act.wait_ge(o_out, 32 * 8)

    @block.vector
    def _(dve):
        v = nc.vector
        total = [0]

        def link(ins_):
            total[0] += 1
            ins_.then_inc(dve_link, 1)
            dve.wait_ge(dve_link, total[0])

        def looped(n, steps, body):
            for i in range(2):
                body(i, link)
            start = total[0]
            if n > 2:
                with dve.Fori(2, n) as i:
                    chain = Chain(dve, dve_link, start + (i - 2) * steps, steps)
                    body(i, chain.link)
                    chain.close()
                total[0] = start + (n - 2) * steps

        v.memset(prm, 0.0).then_inc(params_zeroed, 1)
        dve.wait_ge(cols_pe, 1)
        v.tensor_copy(colp[:, :], bank[2][:, :]).then_inc(cols_dve, 1)
        dve.wait_ge(c_exp, 1)
        link(v.tensor_scalar(sil_e, sil_e, 1.0, None, ALU.add))
        link(v.reciprocal(sil_e, sil_e))
        v.tensor_tensor(sil, colp[:, ds(COLUMN["c"], 32)], sil_e, ALU.mult).then_inc(c_silu, 1)
        for kc in range(DC):
            dve.wait_ge(xt_pe, kc + 1)
            v.tensor_copy(xT[:, kc, :], bank[3 + kc % 3][:, 0:T])
            v.tensor_copy(cxT[:, kc, :], bank[3 + kc % 3][:, T:2 * T]).then_inc(xt_dve, 1)

        def norm_sum_squares(n, squares, width):
            dve.wait_ge(norm_sq, squares)
            v.tensor_reduce(ssq[:, 0:width], hT[:, :, 0:width].rearrange("p c t -> p t c"), AX.X, ALU.add).then_inc(norm_sum, 1)

        def ada_rows(first):
            def body(i):
                for s in range(SLOTS):
                    t = i * SLOTS + first + s
                    dve.wait_ge(ada_used, t + 1)
                    wait(dve, ada_turned, t - 1)
                    v.tensor_copy(arow[0:2, s % 2, :], bank[3 + s % 2][0:2, 0:TILE]).then_inc(ada_row, 1)
            return body

        iterations(dve, ADA_IT, ada_rows(0), 1)
        norm_sum_squares(0, 2, T + TC)
        iterations(dve, ADA_IT, ada_rows(ADA_IT * SLOTS), 1)
        for layer in range(2):
            dve.wait_ge(ada_turned, (layer + 1) * ADA_IT * SLOTS)
            bias = colp[:, ds(COLUMN[f"ada_b{layer}"], 48)].unsqueeze(2).broadcast_to([P, 48, 2])
            v.tensor_tensor(mod[:, layer, :, :], bank[layer][:, 0:96].rearrange("p (a b) -> p a b", b=2), bias,
                            ALU.add).then_inc(mod_ready, 1)
        dve.wait_ge(mod_ready, 2)
        for n, (layer, k) in enumerate(((0, 0), (0, 1), (1, 0))):
            scale = mod[:, layer, DC:2 * DC, k:k + 1].rearrange("p a b -> p (a b)")
            link(v.tensor_scalar(amp[:, n, :], scale, 1.0, None, ALU.add))
            link(v.tensor_tensor(amp[:, n, :], amp[:, n, :], colp[:, ds(COLUMN[f"norm_g{layer}"], DC)], ALU.mult))
        dve.wait_ge(norm_rs, 1)
        for kc in range(DC):
            for k, src in enumerate((xT, cxT)):
                v.scalar_tensor_tensor(out=hT[:, kc, k * T:(k + 1) * T], in0=src[:, kc, :], scalar=amp[:, k, kc:kc + 1],
                                       in1=rs[:, k * T:(k + 1) * T], op0=ALU.mult, op1=ALU.mult).then_inc(norm_mul, 1)

        link(v.tensor_scalar(qg, col("q_g"), ATT, None, ALU.mult))
        na_mask = const("na_mask").unsqueeze(1).broadcast_to([P, 12, NA_COLS])

        def flat(t):
            return t.rearrange("p a b -> p (a b)")

        def na_softmax(a, h, link):
            for qb in range(2):
                dve.wait_ge(na_sc, 4 * a + 2 * h + qb + 1)
                v.tensor_reduce(neg_max[:, qb:qb + 1], bank[3 + qb][:, :], AX.X, ALU.max, negate=True).then_inc(na_max, 1)
            for qb in range(2):
                dve.wait_ge(na_p, 4 * a + 2 * h + qb + 1)
                link(v.reciprocal(row_inv[:, qb:qb + 1], row_sum[:, qb:qb + 1]))
                v.tensor_scalar(prob[:, qb, :], prob[:, qb, :], row_inv[:, qb:qb + 1], None, ALU.mult).then_inc(na_pn, 1)

        def na_turned(a, h):
            dve.wait_ge(na_pt, 2 * a + h + 1)
            wait(dve, na_po, 2 * a + h)
            v.tensor_copy(flat(probT), wide[:, :]).then_inc(na_pts, 1)

        def na_out(a, h):
            dve.wait_ge(na_po, 2 * a + h + 1)
            v.tensor_tensor(chunk(yT, 2 * a + h), bank[5][:, 0:T], gsil[:, h, :], ALU.mult).then_inc(na_y, 1)

        def silu(out_, raw, exp_, link):
            link(v.tensor_scalar(exp_, exp_, 1.0, None, ALU.add))
            link(v.reciprocal(exp_, exp_))
            return v.tensor_tensor(out_, raw, exp_, ALU.mult)

        def na_biases(a):
            dve.wait_ge(na_hk_in, 64 * a + 64)
            f = hankel.rearrange("p a b c -> p (a b) c")
            v.tensor_tensor(f, f, na_mask, ALU.add).then_inc(na_hk, 1)

        def na(i, link):
            a = i - 1
            if not is_first(i):
                na_biases(a)
                na_softmax(a, 0, link)
                na_turned(a, 0)
                na_softmax(a, 1, link)
            dve.wait_ge(na_rs, 3 * i + 1)
            v.scalar_tensor_tensor(out=flat(qhat), in0=flat(qraw), scalar=qg, in1=rsn[:, 0, :], op0=ALU.mult,
                                   op1=ALU.mult).then_inc(na_kq, 1)
            if not is_first(i):
                na_out(a, 0)
                na_turned(a, 1)
                na_out(a, 1)
            dve.wait_ge(acc_free, BANKS["na"] + 6 * i + 2)
            wait(dve, na_y, 2 * i)
            silu(flat(gsil), flat(graw), flat(gexp), link).then_inc(na_g, 1)
            for h in range(2):
                dve.wait_ge(na_rs, 3 * i + 2 + h)
                v.scalar_tensor_tensor(out=khat[:, h, :], in0=kraw[:, h, :], scalar=col("k_g"), in1=rsn[:, 1 + h, :],
                                       op0=ALU.mult, op1=ALU.mult).then_inc(na_kq, 1)

        looped(8, 6, na)
        na_biases(7)
        for h in range(2):
            na_softmax(7, h, link)
            na_turned(7, h)
            na_out(7, h)
        dve.wait_ge(na_y, 16)

        def heads_of(t):
            return t.rearrange("p a (r q) -> p a r q", r=4)

        def conv(g, n, link):
            c = (2 * g, 2 * g + 1, DC + g, DC + 8 + g)[n]
            dve.wait_ge(acc_free, BANKS["ssd"] + 6 * g + n + 1)
            seqs = 2 if n < 3 else 1
            o = acc[:, n % 2, 0:seqs * T].rearrange("p (a b) -> p a b", a=seqs)
            tap = lambda k: pad[:, n % 2, 0:seqs, k:k + T]
            link(v.tensor_scalar(o, tap(0), col("conv_w0", c), col("conv_b", c), ALU.mult, ALU.add))
            for k in range(1, 5):
                last = v.scalar_tensor_tensor(out=o, in0=tap(k), scalar=col(f"conv_w{k}", c), in1=o, op0=ALU.mult,
                                              op1=ALU.add)
                if k < 4:
                    link(last)
            last.then_inc(s_conv, 1)

        def conv_silu(g, n, link):
            dve.wait_ge(s_exp, 4 * g + n + 1)
            for s_, in ((s_xt,),) if n < 2 else (((s_xt,), (s_cb,)) if n == 2 else ((s_ys,),)):
                wait(dve, s_, g)
            width = T + TC if n < 3 else T
            dst = (xc[:, 0, :], xc[:, 1, :], bT, cmT)[n]
            silu(dst, acc[:, n % 2, 0:width], cexp[:, n % 2, 0:width], link).then_inc(s_silu, 1)

        def steps_of_dt():
            dve.wait_ge(ssd_in, 64)
            dve.wait_ge(d_full, 1)
            every = lambda t: t.unsqueeze(1).broadcast_to([P, 4, NDT])
            link(v.tensor_tensor(dt, bank[2][:, 0:4 * NDT].rearrange("p (a b) -> p a b", a=4), every(dbias), ALU.add))
            v.scalar_tensor_tensor(out=flat(dtabs), in0=flat(dt), scalar=-1.0, in1=flat(dt), op0=ALU.mult,
                                   op1=ALU.max).then_inc(d_abs, 1)
            dve.wait_ge(d_log, 1)
            link(v.scalar_tensor_tensor(out=flat(dt), in0=flat(dt), scalar=0.0, in1=flat(dtabs), op0=ALU.max,
                                        op1=ALU.add))
            v.scalar_tensor_tensor(out=dA, in0=dt, scalar=-1.0, in1=every(aneg), op0=ALU.mult, op1=ALU.mult).then_inc(d_a, 1)
            dve.wait_ge(d_csout, 3)
            v.tensor_tensor(toend, toend, dt[:, 2:4, :], ALU.mult).then_inc(d_toend, 1)
            dve.wait_ge(d_toend, 1)

        def to_the_end(s):
            dve.wait_ge(s_xtk, s + 1)
            wait(dve, s_st, s)
            for d in range(2):
                decays = toend[:, :, ds(d * 32 + 4 * s, 4)].unsqueeze(3).broadcast_to([P, 2, 4, 64])
                last = v.tensor_tensor(heads_of(xe[:, d, :, :]), heads_of(xtk[:, 2:4, :]), decays, ALU.mult)
            last.then_inc(s_xe, 1)

        def mask_cb(s, link):
            dve.wait_ge(s_cb, s + 1)
            every = lambda t: t.unsqueeze(1).broadcast_to([P, 2, P])
            v.tensor_tensor(cbf, both_diagonals(bank[2][:, :]), every(LE), ALU.mult)
            link(v.tensor_tensor(cbb, both_diagonals(bank[2][:, :]), every(GE), ALU.mult))

        def decays(s, r):
            if r == 0:
                dve.wait_ge(csb_in, 32 * s + 32)
            wait(dve, s_wm, 4 * s + max(r - 1, 0))
            at = lambda jb, d: cs[:, jb, ds(d * 32 + 4 * s + r, 1)]
            f, b = decay[:, r % 2, 0, :], decay[:, r % 2, 1, :]
            for dst, src, scalar in ((f[:, 0:T], csb[:, 0, r, :], at(0, 0)), (f[:, T:T + P], csb[:, 0, r, P:T], at(1, 0)),
                                     (b[:, 0:P], csb[:, 1, r, 0:P], at(0, 1)), (b[:, P:P + T], csb[:, 1, r, :], at(1, 1))):
                last = v.tensor_scalar(dst, src, scalar, 0.0, ALU.subtract, ALU.min)
            last.then_inc(s_dd, 1)

        def weights(s, r, link):
            dve.wait_ge(s_ed, 4 * s + r + 1)
            wait(dve, s_yi, 4 * s + max(r - 1, 0))
            wait(dve, s_wm, 4 * s + r)
            at = lambda jb, d: dt[:, jb, ds(d * 32 + 4 * s + r, 1)]
            f, b, o, cb = decay[:, r % 2, 0, :], decay[:, r % 2, 1, :], wm[:, r % 2, :], bank[2]
            blk = lambda n: slice(n * P, (n + 1) * P)
            for dst, src, scalar, c in (
                    (o[:, blk(0)], f[:, blk(0)], at(0, 0), cbf[:, 0, :]), (o[:, blk(1)], f[:, blk(1)], at(0, 0), cb[:, blk(1)]),
                    (o[:, blk(3)], f[:, blk(2)], at(1, 0), cbf[:, 1, :]), (wtmp[:, 0, :], b[:, blk(0)], at(0, 1), cbb[:, 0, :]),
                    (o[:, blk(2)], b[:, blk(1)], at(1, 1), cb[:, blk(2)]), (wtmp[:, 1, :], b[:, blk(2)], at(1, 1), cbb[:, 1, :])):
                last = v.scalar_tensor_tensor(out=dst, in0=src, scalar=scalar, in1=c, op0=ALU.mult, op1=ALU.mult)
            link(last)
            v.tensor_tensor(both_diagonals(o), both_diagonals(o), wtmp, ALU.add).then_inc(s_wm, 1)

        def all_heads(s, link):
            decays(s, 0)
            for r in range(1, 4):
                decays(s, r)
                weights(s, r - 1, link)
            weights(s, 3, link)

        def combine(s, link):
            dve.wait_ge(s_ys, s + 1)
            for ib, src in enumerate((bank[5][:, :], wide[:, 0:512])):
                e = ecs[:, ib, :].rearrange("p (d r) -> p d r", d=2)[:, :, ds(4 * s, 4)].unsqueeze(3)
                v.tensor_tensor(heads_of(ysd[:, ib, :, :]), heads_of(src.rearrange("p (a b) -> p a b", a=2)),
                                e.broadcast_to([P, 2, 4, 64]), ALU.mult).then_inc(s_t1, 1)
            dve.wait_ge(s_t1, 2 * s + 2)
            link(v.tensor_tensor(yz, ysd[:, :, 0, :], ysd[:, :, 1, :], ALU.add))
            dve.wait_ge(s_yi, 4 * s + 4)
            link(v.tensor_tensor(flat(yz), flat(yz), bank[4][:, :], ALU.add))
            skip = dskip[:, ds(4 * s, 4)].unsqueeze(2).broadcast_to([P, 4, 64]).unsqueeze(1).broadcast_to([P, 2, 4, 64])
            link(v.tensor_tensor(heads_of(ysd[:, 0, :, :]), heads_of(xtk[:, 0:2, :]), skip, ALU.mult))
            link(v.tensor_tensor(yz, yz, ysd[:, 0, :, :], ALU.add))
            dve.wait_ge(acc_free, BANKS["ssd"] + 6 * s + 6)
            link(silu(flat(zexp), flat(zraw), flat(zexp), link))
            v.tensor_tensor(yz, yz, zexp, ALU.mult).then_inc(s_yz, 1)
            dve.wait_ge(s_rz, s + 1)
            for ib in range(2):
                v.tensor_scalar(yz[:, ib, :], yz[:, ib, :], rz[:, ib:ib + 1], None, ALU.mult).then_inc(s_yn, 1)

        def features(s):
            dve.wait_ge(s_ft, s + 1)
            for c in range(2):
                v.tensor_scalar(chunk(yT, DC + 2 * s + c), bank[3][:, c * T:(c + 1) * T], col("ssd_norm_g", 2 * s + c),
                                None, ALU.mult).then_inc(s_y, 1)

        def ssd(g, link):
            first = is_first(g)
            s = g - 1
            conv(g, 0, link)
            if first:
                steps_of_dt()
            else:
                to_the_end(s)
                mask_cb(s, link)
                all_heads(s, link)
            conv(g, 1, link)
            conv_silu(g, 0, link)
            if not first:
                combine(s, link)
            conv_silu(g, 1, link)
            conv(g, 2, link)
            conv_silu(g, 2, link)
            conv(g, 3, link)
            conv_silu(g, 3, link)
            if not first:
                features(s)
            dve.wait_ge(s_xt, g + 1)
            v.tensor_copy(flat(xtk), wide[:, :])
            v.tensor_copy(flat(btk), bank[5][:, 0:2 * P]).then_inc(s_xtk, 1)

        v.memset(pad, 0.0).then_inc(s_pads, 1)
        looped(8, 16 + 8 + 1 + 4 + 7, ssd)
        to_the_end(7)
        mask_cb(7, link)
        all_heads(7, link)
        combine(7, link)
        features(7)

        def add_out(phase, n, layer):
            per = PHASE[phase][2]

            def body(i, link):
                for b in range(per):
                    k = i * (2 * per) + 2 * b
                    dve.wait_ge(acc_full, BANKS[phase] + i * per + b + 1)
                    for ch in range(2):
                        gate = mod[:, layer, ds(2 * DC + k + ch, 1), 0:1].rearrange("p a b -> p (a b)")
                        last = v.scalar_tensor_tensor(out=chunk(xT, k + ch), in0=bank[b % 2][:, ch * T:(ch + 1) * T],
                                                      scalar=gate, in1=chunk(xT, k + ch), op0=ALU.mult, op1=ALU.add)
                    last.then_inc(acc_free, 1)

            looped(n, 0, body)

        add_out("out", 4, 0)
        norm_sum_squares(1, 3, T)
        dve.wait_ge(norm_rs, 2)
        for kc in range(DC):
            v.scalar_tensor_tensor(out=hT[:, kc, 0:T], in0=xT[:, kc, :], scalar=amp[:, 2, kc:kc + 1], in1=rs[:, 0:T],
                                   op0=ALU.mult, op1=ALU.mult).then_inc(norm_mul, 1)

        link(v.memset(u_pad, 0.0))

        def sc(i, link):
            dve.wait_ge(acc_free, BANKS["sc"] + 4 * i + 3)
            link(v.tensor_tensor(u_pad[:, :, 1:T + 1], u_c, u_h, ALU.mult))
            for k in range(3):
                for ch in range(2):
                    tap, tapw = u_pad[:, ch, k:k + T], col("sc_conv_w", 16 * k + 2 * i + ch)
                    if k == 0:
                        last = v.tensor_scalar(u_out[:, ch, :], tap, tapw, None, ALU.mult)
                    else:
                        last = v.scalar_tensor_tensor(out=u_out[:, ch, :], in0=tap, scalar=tapw, in1=u_out[:, ch, :],
                                                      op0=ALU.mult, op1=ALU.add)
                link(last)
            link(v.tensor_tensor(u_out, u_out, u_b, ALU.mult))
            dve.wait_ge(acc_free, BANKS["sc"] + 4 * i + 4)
            link(silu(u_e, u_g, u_e, link))
            for ch in range(2):
                v.tensor_tensor(chunk(yT, 2 * i + ch), u_out[:, ch, :], u_e[:, ch, :], ALU.mult).then_inc(sc_y, 1)

        looped(8, 8, sc)
        add_out("sco", 2, 1)

        norm_sum_squares(2, 4, T)
        dve.wait_ge(norm_rs, 3)
        for kc in range(DC):
            v.scalar_tensor_tensor(out=hT[:, kc, 0:T], in0=xT[:, kc, :], scalar=col("norm_g_2", kc), in1=rs[:, 0:T],
                                   op0=ALU.mult, op1=ALU.mult).then_inc(norm_out, 1)

        def sb_stays(a, h, link):
            f = 2 * a + h
            dve.wait_ge(sb_log, f + 1)
            wait(dve, sb_w, f)
            link(v.scalar_tensor_tensor(out=stay, in0=bank[3][:, 0:3 * P], scalar=0.0, in1=zlog, op0=ALU.max, op1=ALU.add))
            diag = stay.rearrange("p (a b) -> p a b", a=3)[:, 0:3:2, :]
            v.tensor_tensor(diag, diag, LT.unsqueeze(1).broadcast_to([P, 2, P]), ALU.mult).then_inc(sb_stay, 1)

        def out2(a, h, po, y, base):
            dve.wait_ge(po, 2 * a + h + 1)
            v.tensor_tensor(chunk(yT, base + 2 * a + h), bank[5][:, 0:T], g2sil[:, h, :], ALU.mult).then_inc(y, 1)

        def sbreak(i, link):
            a = i - 1
            if not is_first(i):
                for h in range(2):
                    sb_stays(a, h, link)
                out2(a, 0, sb_po, sb_y, 0)
                out2(a, 1, sb_po, sb_y, 0)
            dve.wait_ge(acc_free, BANKS["sb"] + 4 * i + 2)
            v.tensor_scalar(q2, q2raw, ATT, None, ALU.mult).then_inc(sb_kq, 1)
            v.tensor_copy(k2, k2raw)
            v.tensor_scalar(k2neg, k2raw, -1.0, None, ALU.mult).then_inc(sb_kq, 1)
            dve.wait_ge(acc_free, BANKS["sb"] + 4 * i + 3)
            wait(dve, sb_y, 2 * i)
            silu(flat(g2sil), flat(g2raw), flat(g2exp), link).then_inc(sb_g, 1)

        looped(4, 4, sbreak)
        for h in range(2):
            sb_stays(3, h, link)
            out2(3, h, sb_po, sb_y, 0)
        dve.wait_ge(sb_y, 8)

        v.memset(hank2[64:128, :, T - 64:T], -BIG).then_inc(ch_mask, 1)
        link(v.tensor_scalar(qg2, col("q_g2"), ATT, None, ALU.mult))

        def ch_softmax(a, h, link):
            spans = ((0, P), (P, 3 * P))
            for qb, (lo, hi) in enumerate(spans):
                dve.wait_ge(ch_sc, 4 * a + 2 * h + qb + 1)
                v.tensor_reduce(negmax2[:, qb:qb + 1], bank[3 + qb][:, 0:hi - lo], AX.X, ALU.max,
                                negate=True).then_inc(ch_max, 1)
            for qb, (lo, hi) in enumerate(spans):
                dve.wait_ge(ch_p, 4 * a + 2 * h + qb + 1)
                link(v.reciprocal(rowinv2[:, qb:qb + 1], rowsum2[:, qb:qb + 1]))
                v.tensor_scalar(prob2[:, lo:hi], prob2[:, lo:hi], rowinv2[:, qb:qb + 1], None, ALU.mult).then_inc(ch_pn, 1)

        def ch_turned(a, h):
            dve.wait_ge(ch_pt, 2 * a + h + 1)
            wait(dve, ch_po, 2 * a + h)
            v.tensor_copy(prob2T, wide[:, 0:3 * P]).then_inc(ch_pts, 1)

        def chband(i, link):
            a = i - 1
            if not is_first(i):
                ch_softmax(a, 0, link)
                ch_turned(a, 0)
                ch_softmax(a, 1, link)
                out2(a, 0, ch_po, ch_y, 8)
                ch_turned(a, 1)
                out2(a, 1, ch_po, ch_y, 8)
            for n, (dst, src, g) in enumerate(((q2, q2raw, qg2), (k2, k2raw, col("k_g2")))):
                dve.wait_ge(ch_rs, 2 * i + n + 1)
                v.scalar_tensor_tensor(out=flat(dst), in0=flat(src), scalar=g, in1=rs2[:, n, :], op0=ALU.mult,
                                       op1=ALU.mult).then_inc(ch_kq, 1)
            wait(dve, ch_y, 2 * i)
            silu(flat(g2sil), flat(g2raw), flat(g2exp), link).then_inc(ch_g, 1)

        looped(4, 6, chband)
        for h in range(2):
            ch_softmax(3, h, link)
            ch_turned(3, h)
            out2(3, h, ch_po, ch_y, 8)
        dve.wait_ge(ch_y, 8)

        def last_out(i, link):
            for b in range(4):
                n = 4 * i + b
                dve.wait_ge(acc_full, BANKS["out2"] + n + 1)
                wait(dve, o_tr, n - 1)
                for ch in range(2):
                    last = v.tensor_tensor(o_col[:, b % 2, ch, :], bank[b % 2][:, ch * T:(ch + 1) * T],
                                           chunk(xT, 2 * n + ch), ALU.add)
                last.then_inc(acc_free, 1)

        looped(2, 0, last_out)


_OUT = (1, T, D)


def kernel(**inputs):
    import concourse.bacc as bacc
    from concourse.bass_utils import run_bass_kernel_spmd as run

    nc = bacc.Bacc("TRN2", target_bir_lowering=False, num_devices=1)
    laid = {name: np.ascontiguousarray(a) for name, a in inputs.items()}
    rel = np.zeros(8 * RELN + P, np.float32)
    rel[:8 * RELN] = laid.pop("rel_bias_2")[0][:, ::-1].reshape(-1)
    laid["rel_rev"] = rel
    laid["consts"] = constants()
    arrays, ins = {}, {}
    for name, a in laid.items():
        arrays[f"in_{name}"] = a
        ins[name] = nc.dram_tensor(f"in_{name}", a.shape, mybir.dt.from_np(a.dtype), kind="ExternalInput").ap()
    out = nc.dram_tensor("out_0", _OUT, F32, kind="ExternalOutput").ap()
    scratch = nc.dram_tensor("cs_rows", (NDT, T), F32, kind="Internal").ap()
    build(nc, ins, out, scratch)
    return run(nc, [arrays], core_ids=[0]).results[0]["out_0"]
```
